# Optimizing a Trainium2 kernel written in Bass

```python
import jax, jax.numpy as jnp
from jax import lax
import numpy as np

D_MODEL = 2048
BATCH = 1
SEQ = 256
DEPTH = 2

N_EVEN = (DEPTH + 1) // 2
N_ODD = DEPTH // 2
PLE_DIM = 256
D_FF = 4 * D_MODEL
ROPE_THETA = 10000.0
NORM_EPS = 1e-6
ATTN_Q_BLOCK = 128

MLA_HEADS = 8
MLA_Q_RANK = 512
MLA_KV_RANK = 512
MLA_NOPE = 128
MLA_ROPE = 64
MLA_V = 128
MLA_QK = MLA_NOPE + MLA_ROPE

SWA_HEADS = 16
SWA_KV_HEADS = 2
SWA_HD = 64
SWA_WINDOW = 128
SWA_BLOCK = 128

EVEN_IN_SPLITS = (MLA_Q_RANK, MLA_KV_RANK, MLA_ROPE, SWA_HEADS * SWA_HD, SWA_KV_HEADS * SWA_HD, SWA_KV_HEADS * SWA_HD)
EVEN_IN_WIDTH = sum(EVEN_IN_SPLITS)
EVEN_MIX_WIDTH = MLA_HEADS * MLA_V + SWA_HEADS * SWA_HD

MOBA_HEADS = 16
MOBA_HD = D_MODEL // MOBA_HEADS
MOBA_BLOCK = 256
MOBA_TOPK = 3
MOBA_Q_CHUNK = 32

kernel_name = 'hybrid_mla_swa_moba_sandwich_block'

def rms_norm(t, g):
    tf = t.astype(jnp.float32)
    y = tf * lax.rsqrt(jnp.mean(tf * tf, axis=-1, keepdims=True) + NORM_EPS)
    return (y * g.astype(jnp.float32)).astype(t.dtype)

def apply_rope(t, positions):
    d = t.shape[-1]
    half = d // 2
    inv_freq = jnp.power(ROPE_THETA, -jnp.arange(half, dtype=jnp.float32) * (2.0 / d))
    ang = positions.astype(jnp.float32)[..., None] * inv_freq
    cos = jnp.cos(ang)[:, :, None, :]
    sin = jnp.sin(ang)[:, :, None, :]
    tf = t.astype(jnp.float32)
    t1, t2 = tf[..., :half], tf[..., half:]
    return jnp.concatenate([t1 * cos - t2 * sin, t2 * cos + t1 * sin], axis=-1).astype(t.dtype)

def mla_causal_attention(q_nope, q_rope, k_nope, k_rope, v):
    B, S, H, _ = q_nope.shape
    nb = S // ATTN_Q_BLOCK
    scale = MLA_QK ** -0.5
    qn = q_nope.reshape(B, nb, ATTN_Q_BLOCK, H, MLA_NOPE).transpose(1, 0, 2, 3, 4)
    qr = q_rope.reshape(B, nb, ATTN_Q_BLOCK, H, MLA_ROPE).transpose(1, 0, 2, 3, 4)
    k_idx = jnp.arange(S)

    def one_block(args):
        i, qn_b, qr_b = args
        s = (jnp.einsum('bqhd,bkhd->bhqk', qn_b, k_nope, preferred_element_type=jnp.float32)
             + jnp.einsum('bqhd,bkd->bhqk', qr_b, k_rope, preferred_element_type=jnp.float32)) * scale
        q_idx = i * ATTN_Q_BLOCK + jnp.arange(ATTN_Q_BLOCK)
        s = jnp.where(k_idx[None, :] <= q_idx[:, None], s, -jnp.inf)
        w = jax.nn.softmax(s, axis=-1).astype(v.dtype)
        return jnp.einsum('bhqk,bkhd->bqhd', w, v)

    out = lax.map(one_block, (jnp.arange(nb), qn, qr))
    return out.transpose(1, 0, 2, 3, 4).reshape(B, S, H * MLA_V)

def swa_sink_attention(q, k, v, sinks):
    B, S, HQ, d = q.shape
    G = HQ // SWA_KV_HEADS
    nb = S // SWA_BLOCK
    qb = q.reshape(B, nb, SWA_BLOCK, SWA_KV_HEADS, G, d)
    kb = k.reshape(B, nb, SWA_BLOCK, SWA_KV_HEADS, d)
    vb = v.reshape(B, nb, SWA_BLOCK, SWA_KV_HEADS, d)

    def with_prev(t):
        prev = jnp.pad(t, ((0, 0), (1, 0), (0, 0), (0, 0), (0, 0)))[:, :-1]
        return jnp.concatenate([prev, t], axis=2)

    kw, vw = with_prev(kb), with_prev(vb)
    s = jnp.einsum('bnqkgd,bnjkd->bnkgqj', qb, kw, preferred_element_type=jnp.float32) * (d ** -0.5)
    q_pos = jnp.arange(SWA_BLOCK)[:, None] + SWA_BLOCK
    k_pos = jnp.arange(2 * SWA_BLOCK)[None, :]
    valid = (k_pos <= q_pos) & (q_pos - k_pos < SWA_WINDOW)
    valid_b = valid[None] & ((jnp.arange(nb)[:, None, None] > 0) | (k_pos[None] >= SWA_BLOCK))
    s = jnp.where(valid_b[None, :, None, None], s, -jnp.inf)
    sink = jnp.broadcast_to(sinks.astype(jnp.float32).reshape(SWA_KV_HEADS, G)[None, None, :, :, None, None],
                            s.shape[:-1] + (1,))
    w = jax.nn.softmax(jnp.concatenate([s, sink], axis=-1), axis=-1)[..., :-1].astype(v.dtype)
    o = jnp.einsum('bnkgqj,bnjkd->bnqkgd', w, vw)
    return o.reshape(B, S, HQ * d)

def moba_attention(q, k, v):
    B, S, H, d = q.shape
    pad = (-S) % MOBA_BLOCK
    padw = ((0, 0), (0, pad), (0, 0), (0, 0))
    q, k, v = jnp.pad(q, padw), jnp.pad(k, padw), jnp.pad(v, padw)
    Sp = S + pad
    nkb = Sp // MOBA_BLOCK
    k_sel_n = min(MOBA_TOPK, nkb)
    scale = d ** -0.5
    kb = k.reshape(B, nkb, MOBA_BLOCK, H, d).transpose(0, 3, 1, 2, 4)
    vb = v.reshape(B, nkb, MOBA_BLOCK, H, d).transpose(0, 3, 1, 2, 4)
    k_mean = jnp.mean(kb.astype(jnp.float32), axis=3)
    gate = jnp.einsum('bshd,bhnd->bhsn', q.astype(jnp.float32), k_mean)
    q_blk = jnp.arange(Sp) // MOBA_BLOCK
    fully_past = jnp.arange(nkb)[None, :] < q_blk[:, None]
    gate = jnp.where(fully_past[None, None], gate, -jnp.inf)
    top_val, top_idx = lax.top_k(gate, k_sel_n)
    sel_ok = jnp.isfinite(top_val)
    C = MOBA_Q_CHUNK
    nq = Sp // C
    qc = q.reshape(B, nq, C, H, d).transpose(1, 0, 2, 3, 4)
    idx_c = top_idx.reshape(B, H, nq, C, k_sel_n).transpose(2, 0, 1, 3, 4)
    ok_c = sel_ok.reshape(B, H, nq, C, k_sel_n).transpose(2, 0, 1, 3, 4)
    b_ix = jnp.arange(B)[:, None, None, None]
    h_ix = jnp.arange(H)[None, :, None, None]

    def one_chunk(args):
        ci, q_c, idx, ok = args
        start = ci * C
        blk = start // MOBA_BLOCK
        k_g = kb[b_ix, h_ix, idx]
        v_g = vb[b_ix, h_ix, idx]
        s_sel = jnp.einsum('bqhd,bhqkjd->bhqkj', q_c, k_g, preferred_element_type=jnp.float32) * scale
        s_sel = jnp.where(ok[..., None], s_sel, -jnp.inf).reshape(B, H, C, k_sel_n * MOBA_BLOCK)
        own_k = lax.dynamic_index_in_dim(kb, blk, axis=2, keepdims=False)
        own_v = lax.dynamic_index_in_dim(vb, blk, axis=2, keepdims=False)
        s_own = jnp.einsum('bqhd,bhjd->bhqj', q_c, own_k, preferred_element_type=jnp.float32) * scale
        q_pos = start + jnp.arange(C)
        k_pos = blk * MOBA_BLOCK + jnp.arange(MOBA_BLOCK)
        s_own = jnp.where(k_pos[None, :] <= q_pos[:, None], s_own, -jnp.inf)
        w = jax.nn.softmax(jnp.concatenate([s_sel, s_own], axis=-1), axis=-1).astype(v.dtype)
        w_sel = w[..., :k_sel_n * MOBA_BLOCK].reshape(B, H, C, k_sel_n, MOBA_BLOCK)
        w_own = w[..., k_sel_n * MOBA_BLOCK:]
        return (jnp.einsum('bhqkj,bhqkjd->bqhd', w_sel, v_g)
                + jnp.einsum('bhqj,bhjd->bqhd', w_own, own_v))

    o = lax.map(one_chunk, (jnp.arange(nq), qc, idx_c, ok_c))
    return o.transpose(1, 0, 2, 3, 4).reshape(B, Sp, H * d)[:, :S]

def even_mixer(h, positions, w_in, q_norm_g, w_q_up, kv_norm_g, w_kv_up, sinks, w_out):
    B, S, _ = h.shape
    proj = h @ w_in
    offs = np.cumsum(EVEN_IN_SPLITS)[:-1].tolist()
    cq, ckv, k_rope, q_s, k_s, v_s = jnp.split(proj, offs, axis=-1)
    q = (rms_norm(cq, q_norm_g) @ w_q_up).reshape(B, S, MLA_HEADS, MLA_QK)
    q_nope = q[..., :MLA_NOPE]
    q_rope = apply_rope(q[..., MLA_NOPE:], positions)
    kv = (rms_norm(ckv, kv_norm_g) @ w_kv_up).reshape(B, S, MLA_HEADS, MLA_NOPE + MLA_V)
    k_nope, v_mla = kv[..., :MLA_NOPE], kv[..., MLA_NOPE:]
    k_rope = apply_rope(k_rope[:, :, None, :], positions)[:, :, 0, :]
    o_mla = mla_causal_attention(q_nope, q_rope, k_nope, k_rope, v_mla)
    q_s = apply_rope(q_s.reshape(B, S, SWA_HEADS, SWA_HD), positions)
    k_s = apply_rope(k_s.reshape(B, S, SWA_KV_HEADS, SWA_HD), positions)
    v_s = v_s.reshape(B, S, SWA_KV_HEADS, SWA_HD)
    o_swa = swa_sink_attention(q_s, k_s, v_s, sinks)
    return jnp.concatenate([o_mla, o_swa], axis=-1) @ w_out

def odd_mixer(h, positions, w_qkv, w_out):
    B, S, _ = h.shape
    q, k, v = jnp.split(h @ w_qkv, 3, axis=-1)
    q = apply_rope(q.reshape(B, S, MOBA_HEADS, MOBA_HD), positions)
    k = apply_rope(k.reshape(B, S, MOBA_HEADS, MOBA_HD), positions)
    v = v.reshape(B, S, MOBA_HEADS, MOBA_HD)
    return moba_attention(q, k, v) @ w_out

def sq_relu_mlp(h, w_up, w_down):
    a = jax.nn.relu(h @ w_up)
    return (a * a) @ w_down

def setup_inputs(seed: int = 0) -> dict:
    key = jax.random.key(seed)
    ks = iter(jax.random.split(key, 32))

    def w(shape, fan_in):
        return jax.random.normal(next(ks), shape, jnp.float32) * (fan_in ** -0.5)

    def gain(shape):
        return 1.0 + 0.05 * jax.random.normal(next(ks), shape, jnp.float32)

    x = jax.random.normal(next(ks), (BATCH, SEQ, D_MODEL), jnp.float32)
    p = jax.random.normal(next(ks), (DEPTH, BATCH, SEQ, PLE_DIM), jnp.float32)
    positions = jnp.broadcast_to(jnp.arange(SEQ, dtype=jnp.int32)[None, :], (BATCH, SEQ))
    return {
        'x': x,
        'p': p,
        'positions': positions,
        'even_pre_g': gain((N_EVEN, D_MODEL)),
        'even_w_in': w((N_EVEN, D_MODEL, EVEN_IN_WIDTH), D_MODEL),
        'mla_q_norm_g': gain((N_EVEN, MLA_Q_RANK)),
        'mla_w_q_up': w((N_EVEN, MLA_Q_RANK, MLA_HEADS * MLA_QK), MLA_Q_RANK),
        'mla_kv_norm_g': gain((N_EVEN, MLA_KV_RANK)),
        'mla_w_kv_up': w((N_EVEN, MLA_KV_RANK, MLA_HEADS * (MLA_NOPE + MLA_V)), MLA_KV_RANK),
        'swa_sinks': jax.random.normal(next(ks), (N_EVEN, SWA_HEADS), jnp.float32),
        'even_w_out': w((N_EVEN, EVEN_MIX_WIDTH, D_MODEL), EVEN_MIX_WIDTH),
        'even_post_g': gain((N_EVEN, D_MODEL)),
        'odd_pre_g': gain((N_ODD, D_MODEL)),
        'moba_w_qkv': w((N_ODD, D_MODEL, 3 * MOBA_HEADS * MOBA_HD), D_MODEL),
        'odd_w_out': w((N_ODD, MOBA_HEADS * MOBA_HD, D_MODEL), MOBA_HEADS * MOBA_HD),
        'odd_post_g': gain((N_ODD, D_MODEL)),
        'mlp_pre_g': gain((DEPTH, D_MODEL)),
        'mlp_w_up': w((DEPTH, D_MODEL, D_FF), D_MODEL),
        'mlp_w_down': w((DEPTH, D_FF, D_MODEL), D_FF),
        'mlp_post_g': gain((DEPTH, D_MODEL)),
        'ple_w_gate': w((DEPTH, D_MODEL, D_MODEL), D_MODEL),
        'ple_b_gate': 0.02 * jax.random.normal(next(ks), (DEPTH, D_MODEL), jnp.float32),
        'ple_w_proj': w((DEPTH, PLE_DIM, D_MODEL), PLE_DIM),
    }

def reference(x, p, positions, even_pre_g, even_w_in, mla_q_norm_g, mla_w_q_up, mla_kv_norm_g,
              mla_w_kv_up, swa_sinks, even_w_out, even_post_g, odd_pre_g, moba_w_qkv, odd_w_out,
              odd_post_g, mlp_pre_g, mlp_w_up, mlp_w_down, mlp_post_g, ple_w_gate, ple_b_gate,
              ple_w_proj):
    h = x
    for i in range(DEPTH):
        j = i // 2
        if i % 2 == 0:
            m = even_mixer(rms_norm(h, even_pre_g[j]), positions, even_w_in[j], mla_q_norm_g[j],
                           mla_w_q_up[j], mla_kv_norm_g[j], mla_w_kv_up[j], swa_sinks[j], even_w_out[j])
            h = h + rms_norm(m, even_post_g[j])
        else:
            m = odd_mixer(rms_norm(h, odd_pre_g[j]), positions, moba_w_qkv[j], odd_w_out[j])
            h = h + rms_norm(m, odd_post_g[j])
        f = sq_relu_mlp(rms_norm(h, mlp_pre_g[i]), mlp_w_up[i], mlp_w_down[i])
        h = h + rms_norm(f, mlp_post_g[i])
        gate = jax.nn.sigmoid(h @ ple_w_gate[i] + ple_b_gate[i])
        h = h + gate * (p[i] @ ple_w_proj[i])
    return h


_drawn_inputs = setup_inputs


def setup_inputs(seed=0):
    import zlib

    import numpy as np

    out = dict(_drawn_inputs(seed))
    spreads = {}
    factors = {'mla_q_norm_g': 2.698, 'swa_sinks': 2.885, 'ple_b_gate': 24.48}
    for name, (base, spread) in spreads.items():
        noise = np.random.default_rng([zlib.crc32(name.encode()), seed]).standard_normal(out[name].shape)
        drawn = base * np.exp(spread * noise) if base else spread * noise
        out[name] = __import__('jax').numpy.asarray(drawn.astype(out[name].dtype))
    for name, factor in factors.items():
        out[name] = (out[name] * factor).astype(out[name].dtype)
    return out
```

```python
from contextlib import ExitStack, contextmanager

import numpy as np
import concourse.bass as bass
from concourse import mybir

ALU = mybir.AluOpType
ACT = mybir.ActivationFunctionType
AX = mybir.AxisListType.X
F32 = mybir.dt.float32
F32R = mybir.dt.float32r
I32 = mybir.dt.int32

P = 128
HALVES = 2
SEQ = P * HALVES
D = 2048
KT = D // P
CW = 512
CHUNKS = D // CW
DFF = 4 * D
GROUPS = DFF // D
EPS = 1e-6
THETA = 10000.0
RAW = 4
RING = 8
MLA_H, NOPE, ROPE, RANK = 8, 128, 64, 512
SWA_H, SWA_KV, SWA_D = 16, 2, 64
MOBA_H, MOBA_D = 16, 128
PLE = 256
NEG = -3.0e38
TWO_PI = 2.0 * np.pi
PI_A = 6.28125
PI_B = float(np.float32(np.float32((TWO_PI - PI_A) * 2**21).round() / 2**21))
PI_C = float(TWO_PI - PI_A - PI_B)
PI_MAX = 3.1415925

IN_WIDTHS = (512, 512, 512, 512, 320)
Q_UP_W = 2 * (NOPE + ROPE)
PAIRS = (5 * 8 + 4 * 2 + 4 * 2 + 4 * 8 + GROUPS * 8 * 8 + 4 + 4 * 8
         + 12 * 8 + 4 * 8 + GROUPS * 8 * 8 + 4 + 4 * 8)
ROWS_BEFORE_GATE = (3 * 2 + 4 * 2 + GROUPS * 4 * 2, 3 * 2 + 4 * 2 + GROUPS * 4 * 2 + 8 + 8 * 2 + GROUPS * 4 * 2)


class Count:

    def __init__(self, base=0):
        self.base, self.terms = base, []

    def add(self, n=1):
        self.base += n
        return self.at()

    def at(self, plus=0):
        value = self.base + plus
        for reg, step in self.terms:
            value = reg * step + value
        return value


@contextmanager
def repeat(eng, times, steps):
    with eng.Fori(0, times) as i:
        before = {c: c.base for c in steps}
        for c, step in steps.items():
            c.terms.append((i, step))
        yield i
        for c, step in steps.items():
            assert c.base - before[c] == step, (c.base - before[c], step)
            c.terms.pop()
    for c, step in steps.items():
        c.base += (times - 1) * step


def build(nc, x, x_t, p_t, pos, gains_t, rows, sinks, freqs, w_stream, out):
    ctx = ExitStack()
    with ctx:
        def sb(name, shape, dt=F32):
            return ctx.enter_context(nc.sbuf_tensor(name, shape, dt))

        def sem(name):
            return ctx.enter_context(nc.semaphore(name))

        with nc.sbuf_tensor("mla_q_swa_kv", [P, 4096], F32) as over_m, \
                nc.sbuf_tensor("mla_k_swa_q", [P, 4096], F32) as over_a:
            pass
        with nc.sbuf_tensor("spacer", [P, 4096], F32), \
                nc.sbuf_tensor("moba_qk", [P, 8192], F32) as over_qk:
            pass
        m = sb("mixed", [P, HALVES, D])
        ah = sb("hidden_hi", [P, KT, SEQ], F32R)
        al = sb("hidden_lo", [P, KT, SEQ], F32R)
        xh = sb("act_hi", [P, KT, SEQ], F32R)
        xl = sb("act_lo", [P, KT, SEQ], F32R)
        h = sb("residual", [P, HALVES, D])
        raw = sb("w_raw", [P, RAW, 2 * CW])
        wh = sb("w_hi", [P, RING, 2 * CW], F32R)
        wl = sb("w_lo", [P, RING, 2 * CW], F32R)
        vm = sb("mla_v_ple", [P, HALVES, MLA_H * 128])
        gbc = sb("row_bc", [P, D])
        row = sb("row", [P, HALVES, CW])
        tmp = sb("tmp", [P, CW])
        ident = sb("ident", [P, P])
        mask_causal = sb("mask_causal", [P, 3 * P])
        mask_window = sb("mask_window", [P, 3 * P])
        cos64 = sb("cos64", [P, HALVES, 32])
        sin64 = sb("sin64", [P, HALVES, 2, 32])
        cos128 = sb("cos128", [P, HALVES, 64])
        sin128 = sb("sin128", [P, HALVES, 2, 64])
        gt = sb("gains_k", [P, 72])
        stats = sb("stats", [P, 128])
        nsink = sb("neg_sinks", [P, 2 * SWA_H])
        pos_i = sb("pos_i", [P, HALVES], I32)
        ps = ctx.enter_context(nc.psum_tensor("banks", [P, 8, CW], F32))
        G, T, L, JUNK = (0, 1), (2, 3), (4, 5), 7

        mla_q = over_m[:, 0:3072].rearrange("p (c b t) -> p c b t", c=4, b=3)
        swa_k = over_m[:, 3072:3840].rearrange("p (b t) -> p b t", b=3)
        swa_v = over_m[:, 3840:4096].rearrange("p (t c) -> p t c", t=2)
        mla_k = over_a[:, 0:2048].rearrange("p (b t) -> p b t", b=8)
        swa_q = over_a[:, 2048:4096].rearrange("p (b t) -> p b t", b=8)
        moba_qk = over_qk[:, :].rearrange("p (b t) -> p b t", b=32)
        x_raw = m[:, :, :].rearrange("p t (k s) -> p (t k) s", s=SEQ)
        p_raw = tmp[:, :].rearrange("p (k s) -> p k s", k=2)
        proj1 = vm[:, :, :].rearrange("p t c -> p (t c)")
        prob = [gbc[:, 384 * i:384 * i + 384] for i in range(3)]
        prob_t = [gbc[:, 1152 + 384 * i:1536 + 384 * i] for i in range(2)]
        doubled = [gbc[:, 384 * t:384 * t + 384] for t in range(HALVES)]
        sinkv = nsink[:, SWA_H:2 * SWA_H]

        def ssq(norm, t, a=0, b=4):
            return stats[:, 10 * norm + 5 * t + a:10 * norm + 5 * t + b]

        def rstd(norm, t):
            return stats[:, 10 * norm + 5 * t + 4:10 * norm + 5 * t + 5]

        N_PRE0, N_Q, N_KV, N_POST0, N_MPRE0, N_MPOST0, N_PRE1, N_POST1, N_MPRE1, N_MPOST1 = range(10)
        var, std, rec, cor = (stats[:, 100 + i:101 + i] for i in range(4))
        nmax = [stats[:, 104 + 2 * i:106 + 2 * i] for i in range(3)]
        rsum = [stats[:, 110 + 2 * i:112 + 2 * i] for i in range(3)]
        esink = [stats[:, 116 + 2 * i:118 + 2 * i] for i in range(3)]
        rinv = [stats[:, 122 + 2 * i:124 + 2 * i] for i in range(3)]

        raw_loaded = [sem(f"raw_loaded{i}") for i in range(RAW)]
        tables_loaded, x_loaded, p_loaded = sem("tables_loaded"), sem("x_loaded"), sem("p_loaded")
        xt_loaded = [sem(f"xt_loaded{i}") for i in range(4)]
        row_bc_loaded = sem("row_bc_loaded")
        out_stored = [sem(f"out_stored{t}") for t in range(HALVES)]
        w_hi_ready, w_lo_ready = sem("w_hi_ready"), sem("w_lo_ready")
        w_used = sem("w_used")
        half0_done = sem("half0_done")
        bank_free = [sem(f"bank_free{t}") for t in range(HALVES)]
        row_done = sem("row_done")
        sq_done = sem("sq_done")
        h_ready = sem("h_ready")
        h_saved = sem("h_saved")
        split_t_done = sem("split_t_done")
        split_hi_done, split_lo_done = sem("split_hi_done"), sem("split_lo_done")
        plain_t_done, plain_copied = sem("plain_t_done"), sem("plain_copied")
        var_ready, std_ready, rstd_ready = sem("var_ready"), sem("std_ready"), sem("rstd_ready")
        consts_ready = sem("consts_ready")
        angles_ready, sines_ready = sem("angles_ready"), sem("sines_ready")
        x_hi, x_lo, p_hi, p_lo = sem("x_hi"), sem("x_lo"), sem("p_hi"), sem("p_lo")
        m_zeroed = sem("m_zeroed")
        sig_done = sem("sig_done")
        s_done, s_masked, nmax_ready = sem("s_done"), sem("s_masked"), sem("nmax_ready")
        exp_done, p_ready = sem("exp_done"), sem("p_ready")
        pt_done, pt_copied, o_done = sem("pt_done"), sem("pt_copied"), sem("o_done")
        o_hi, o_lo = sem("o_hi"), sem("o_lo")
        act_step, dve_step, pool_step = sem("act_step"), sem("dve_step"), sem("pool_step")

        block = ctx.enter_context(nc.Block())

        @block.sync
        def _(sp):
            sp.dma_start(gt[:], gains_t).then_inc(tables_loaded, 16)
            sp.dma_start(pos_i[:], pos).then_inc(tables_loaded, 16)
            sp.dma_start(tmp[:, 0:96], freqs.partition_broadcast(P)).then_inc(tables_loaded, 16)
            sp.dma_start(nsink[:, SWA_H:2 * SWA_H], sinks.partition_broadcast(P)).then_inc(tables_loaded, 16)
            for n in range(RAW):
                sp.dma_start(x_raw[:, 4 * n:4 * n + 4, :], x_t[:, 4 * n:4 * n + 4, :]).then_inc(xt_loaded[n], 16)
                sp.dma_start(raw[:, n, :], w_stream[n]).then_inc(raw_loaded[n], 16)
            sp.dma_start(h[:, :, :], x.rearrange("(t p) d -> p t d", p=P)).then_inc(x_loaded, 16)
            with sp.Fori(1, PAIRS // RAW) as i:
                for n in range(RAW):
                    sp.wait_ge(w_lo_ready, i * RAW + (n - RAW + 1))
                    sp.dma_start(raw[:, n, :], w_stream[i * RAW + n]).then_inc(raw_loaded[n], 16)

        @block.gpsimd
        def _(pool):
            steps = Count()

            def link(ins):
                ins.then_inc(pool_step, 1)
                pool.wait_ge(pool_step, steps.add())

            link(pool.memset(ident[:, :], 0.0))
            pool.affine_select(out=ident[:, :], in_=ident[:, :], compare_op=ALU.not_equal, fill=1.0,
                               base=0, pattern=[[-1, P]], channel_multiplier=1).then_inc(consts_ready, 1)
            link(pool.memset(mask_causal[:, :], 0.0))
            link(pool.memset(mask_window[:, :], 0.0))
            for k, mask in enumerate((mask_causal, mask_causal, mask_window, mask_window)):
                part = mask[:, (k % 2) * 2 * P:(k % 2) * 2 * P + P]
                pool.affine_select(out=part, in_=part, compare_op=ALU.is_ge, fill=NEG, base=0,
                                   pattern=[[-1, P]], channel_multiplier=1).then_inc(consts_ready, 1)
            part = mask_window[:, P:2 * P]
            pool.affine_select(out=part, in_=part, compare_op=ALU.is_gt, fill=NEG, base=0,
                               pattern=[[1, P]], channel_multiplier=-1).then_inc(consts_ready, 1)

            for layer in range(2):
                heads = (MLA_H + SWA_H // 2, MLA_H + SWA_H // 2 + MOBA_H)[layer]
                pool.wait_ge(o_lo, heads)
                pool.dma_start(gbc[:, :], rows[3 * layer].partition_broadcast(P)).then_inc(row_bc_loaded, 16)
                pool.wait_ge(h_ready, 16 * layer + 8)
                link(pool.memset(m[:, 0, :], 0.0))
                pool.memset(m[:, 1, :], 0.0).then_inc(m_zeroed, 1)
                pool.dma_start(gbc[:, :], rows[3 * layer + 1].partition_broadcast(P)).then_inc(row_bc_loaded, 16)
                pool.dma_start(p_raw, p_t[layer]).then_inc(p_loaded, 16)
                pool.wait_ge(h_ready, 16 * layer + 16)
                pool.dma_start(gbc[:, :], rows[3 * layer + 2].partition_broadcast(P)).then_inc(row_bc_loaded, 16)
            for c in range(CHUNKS):
                for t in range(HALVES):
                    pool.wait_ge(row_done, ROWS_BEFORE_GATE[1] + HALVES * c + t + 1)
                    pool.dma_start(out[t * P:(t + 1) * P, c * CW:(c + 1) * CW], row[:, t, :]).then_inc(out_stored[t], 16)
            for t in range(HALVES):
                pool.wait_ge(out_stored[t], 16 * CHUNKS)

        @block.tensor
        def _(pe):
            lo_seen, used, half0 = Count(), Count(), Count()
            jobs = [Count(), Count()]
            rows_seen, h_seen = Count(), Count()
            split_n, plain_n = Count(), Count()
            slot = [0]
            bank_parity = {"split": 0, "plain": 0}

            def job(t, hi, lo, pairs, width=CW, keep=False, need=None, after=None):
                if jobs[t].base:
                    pe.wait_ge(bank_free[t], jobs[t].at())
                jobs[t].add()
                tok = slice(t * P, (t + 1) * P)
                acc = ps[:, G[t], 0:width]
                for j in range(pairs):
                    s = (slot[0] + j) % RING
                    if t == 0:
                        pe.wait_ge(w_lo_ready, lo_seen.add())
                    if need and j in need:
                        pe.wait_ge(*need[j])
                    for k in range(2):
                        cols = slice(k * CW, k * CW + width)
                        kt = 2 * j + k
                        for n, (a, w) in enumerate(((hi, wh), (hi, wl), (lo, wh))):
                            last = pe.matmul(acc, a[:, kt, tok], w[:, s, cols],
                                             start=(kt == 0 and n == 0), stop=(kt == 2 * pairs - 1 and n == 2))
                    if t == 1:
                        last.then_inc(w_used, 1)
                        used.add()
                    elif j == pairs - 1:
                        last.then_inc(half0_done, 1)
                        half0.add()
                    if after and j in after:
                        after[j]()
                if t == 1:
                    slot[0] = (slot[0] + pairs) % RING

            def split_transpose(src, blocks=4):
                if split_n.base >= 2:
                    pe.wait_ge(split_lo_done, split_n.at(-1))
                b = T[split_n.base % 2]
                for i in range(blocks):
                    last = pe.transpose(ps[:, b, i * P:(i + 1) * P], src[:, i * P:(i + 1) * P], ident[:, :])
                last.then_inc(split_t_done, 1)
                split_n.add()

            def plain_transpose(src, blocks=4):
                if plain_n.base >= 2:
                    pe.wait_ge(plain_copied, plain_n.at(-1))
                b = L[plain_n.base % 2]
                for i in range(blocks):
                    last = pe.transpose(ps[:, b, i * P:(i + 1) * P], src[:, i * P:(i + 1) * P], ident[:, :])
                last.then_inc(plain_t_done, 1)
                plain_n.add()

            def row_split(t, blocks=4):
                pe.wait_ge(row_done, rows_seen.add())
                split_transpose(row[:, t, :], blocks)

            def row_plain(t, blocks=4, src=None):
                pe.wait_ge(row_done, rows_seen.add())
                plain_transpose(row[:, t, :] if src is None else src, blocks)

            def evacuated(t):
                pe.wait_ge(bank_free[t], jobs[t].at())

            def up_turn(c, t):
                if c < 4:
                    row_plain(t, 3)
                else:
                    evacuated(t)
                    plain_transpose(row[:, t, :], 2)

            def h_piece(t, i):
                pe.wait_ge(h_ready, h_seen.add())
                split_transpose(h[:, t, i * CW:(i + 1) * CW])

            def pieces(t):
                return {4 + i: (lambda i=i: h_piece(t, i)) for i in range(4)}

            def pieces_ready(first):
                return {2 * i: (split_lo_done, first + i + 1) for i in range(4)}

            loop_counts = lambda extra, n=1: {lo_seen: 8 * n, used: 8 * n, half0: n, jobs[0]: n, jobs[1]: n, **extra}

            pe.wait_ge(consts_ready, 1)
            for c in range(5):
                def turn_previous(c=c):
                    if c == 0:
                        return
                    if c - 1 < 2:
                        pe.wait_ge(bank_free[1], c)
                        split_transpose(row[:, 1, :])
                    else:
                        row_plain(1)

                def turn_this(c=c):
                    if c < 2:
                        evacuated(0)
                        split_transpose(row[:, 0, :])
                    elif c < 4:
                        row_plain(0)
                    else:
                        row_plain(0, 3, doubled[0])
                need = {2 * i: (x_lo, 4 * i + 4) for i in range(4)} if c == 0 else None
                job(0, xh, xl, 8, IN_WIDTHS[c], need=need, after={5: turn_previous})
                job(1, xh, xl, 8, IN_WIDTHS[c], after={5: turn_this})

            q_latent = (al[:, 0:4, :], al[:, 4:8, :])
            kv_latent = (al[:, 8:12, :], al[:, 12:16, :])
            for c in range(8):
                lhs, width = (q_latent, Q_UP_W) if c < 4 else (kv_latent, CW)
                need = {0: (split_lo_done, 2 if c < 4 else 4)} if c % 4 == 0 else None
                job(0, *lhs, 2, width, need=need)
                if c == 0:
                    row_plain(1, 3, doubled[1])
                elif c - 1 < 4:
                    row_plain(1, 3)
                else:
                    pe.wait_ge(bank_free[1], 5 + c)
                    plain_transpose(row[:, 1, :], 2)
                job(1, *lhs, 2, width)
                up_turn(c, 0)
            up_turn(7, 1)

            def scores(n, q_parts, k_parts):
                if n >= 2:
                    pe.wait_ge(s_masked, n - 1)
                for a, b, keys in ((0, P, P), (P, 3 * P, 2 * P)):
                    tok = slice(0, P) if a == 0 else slice(P, 2 * P)
                    for i, (q, k) in enumerate(zip(q_parts, k_parts)):
                        last = pe.matmul(ps[:, L[n % 2], a:b], q[:, tok], k[:, 0:keys],
                                         start=(i == 0), stop=(i == len(q_parts) - 1))
                last.then_inc(s_done, 1)

            def turn_probs(n):
                pe.wait_ge(p_ready, n + 1)
                if n >= 2:
                    pe.wait_ge(pt_copied, n - 1)
                for i in range(3):
                    last = pe.transpose(ps[:, T[n % 2], i * P:(i + 1) * P], prob[n % 3][:, i * P:(i + 1) * P], ident[:, :])
                last.then_inc(pt_done, 1)

            def values(n, v, part, o_bank, o_wait):
                pe.wait_ge(pt_copied, n + 1)
                if o_wait:
                    pe.wait_ge(o_lo, o_wait)
                pe.matmul(ps[part, G[o_bank], 0:SEQ], v(0), prob_t[n % 2][:, 0:SEQ], start=True, stop=False)
                last = pe.matmul(ps[part, G[o_bank], P:SEQ], v(1), prob_t[n % 2][:, SEQ:SEQ + P], start=False, stop=True)
                last.then_inc(o_done, 1)

            def attention(first, heads):
                for i in range(len(heads) + 2):
                    if i < len(heads):
                        scores(first + i, heads[i][0], heads[i][1])
                    if i >= 2:
                        values(first + i - 2, *heads[i - 2][2:])
                    if 1 <= i <= len(heads):
                        turn_probs(first + i - 1)

            pe.wait_ge(plain_copied, plain_n.at())
            pe.wait_ge(bank_free[0], jobs[0].at())
            pe.wait_ge(bank_free[1], jobs[1].at())
            pe.wait_ge(split_lo_done, split_n.at())
            heads = []
            for hd in range(MLA_H):
                part = slice(64 * (hd % 2), 64 * (hd % 2) + 64)
                heads.append(((mla_q[:, hd // 2, hd % 2, :], mla_q[part, hd // 2, 2, :]),
                              (mla_k[:, hd, :], swa_k[part, 2, :]),
                              lambda blk, hd=hd: vm[:, blk, hd * 128:hd * 128 + 128],
                              slice(0, P), hd % 2, max(0, hd - 1)))
            for hd in range(SWA_H):
                part = slice(64 * (hd % 2), 64 * (hd % 2) + 64)
                kv = hd // (SWA_H // SWA_KV)
                pair = MLA_H + hd // 2
                heads.append(((swa_q[part, hd // 2, :],), (swa_k[part, kv, :],),
                              lambda blk, kv=kv: swa_v[:, blk, kv * 64:kv * 64 + 64],
                              part, pair % 2, pair - 1))
            attention(0, heads)

            def mixer_out_and_mlp(layer):
                with repeat(pe, 3, loop_counts({})):
                    job(0, xh, xl, 8)
                    job(1, xh, xl, 8)
                job(0, xh, xl, 8)
                s0 = split_n.at()
                job(1, xh, xl, 8, after=pieces(0))
                job(0, xh, xl, 8, need=pieces_ready(s0), after=pieces(1))
                job(1, xh, xl, 8, need=pieces_ready(s0 + 4), after={2: lambda: row_split(0)})

                def up_rest():
                    with repeat(pe, 3, loop_counts({split_n: 2, rows_seen: 2})):
                        job(0, xh, xl, 8, after={2: lambda: row_split(1)})
                        job(1, xh, xl, 8, after={2: lambda: row_split(0)})

                def down(times, first):
                    if first:
                        n = split_n.at()
                        job(0, ah, al, 8, need={6: (split_lo_done, n)}, after={2: lambda: row_split(1)})
                        job(1, ah, al, 8, need={6: (split_lo_done, split_n.at())})
                    with repeat(pe, times, loop_counts({})):
                        job(0, ah, al, 8)
                        job(1, ah, al, 8)

                with repeat(pe, 3, loop_counts({split_n: 8, rows_seen: 8}, 8)):
                    up_rest()
                    down(3, True)
                    job(0, xh, xl, 8)
                    job(1, xh, xl, 8, after={2: lambda: row_split(0)})
                up_rest()
                down(2, True)
                job(0, ah, al, 8)
                s1 = split_n.at()
                job(1, ah, al, 8, after=pieces(0))
                pe.wait_ge(p_lo, layer + 1)
                for c in range(CHUNKS):
                    job(0, xh, xl, 1)
                    job(1, xh, xl, 1)
                turn = layer == 0
                job(0, ah, al, 8, need=pieces_ready(s1), after=pieces(1))
                job(1, ah, al, 8, need=pieces_ready(s1 + 4), after={5: lambda: row_split(0)} if turn else None)
                with repeat(pe, 3, loop_counts({split_n: 2, rows_seen: 2} if turn else {})):
                    job(0, ah, al, 8, after={5: lambda: row_split(1)} if turn else None)
                    job(1, ah, al, 8, after={5: lambda: row_split(0)} if turn else None)

            pe.wait_ge(o_lo, MLA_H + SWA_H // 2)
            mixer_out_and_mlp(0)

            n = split_n.at()
            job(0, xh, xl, 8, need={6: (split_lo_done, n)}, after={2: lambda: row_split(1)})
            job(1, xh, xl, 8, need={6: (split_lo_done, split_n.at())}, after={5: lambda: row_plain(0)})
            with repeat(pe, 7, loop_counts({plain_n: 2, rows_seen: 2})):
                job(0, xh, xl, 8, after={5: lambda: row_plain(1)})
                job(1, xh, xl, 8, after={5: lambda: row_plain(0)})
            job(0, xh, xl, 8, after={5: lambda: row_plain(1)})
            job(1, xh, xl, 8)
            with repeat(pe, 3, loop_counts({})):
                job(0, xh, xl, 8)
                job(1, xh, xl, 8)
            pe.wait_ge(plain_copied, plain_n.at())
            pe.wait_ge(bank_free[0], jobs[0].at())
            pe.wait_ge(bank_free[1], jobs[1].at())
            n0 = MLA_H + SWA_H
            o0 = MLA_H + SWA_H // 2
            attention(n0, [((moba_qk[:, hd, :],), (moba_qk[:, MOBA_H + hd, :],),
                            lambda blk, hd=hd: m[:, blk, hd * 128:hd * 128 + 128],
                            slice(0, P), hd % 2, o0 + hd - 1) for hd in range(MOBA_H)])
            pe.wait_ge(o_lo, o0 + MOBA_H)
            mixer_out_and_mlp(1)

        @block.scalar
        def _(act):
            conv, half0, used, sq, split_n, plain_n = (Count() for _ in range(6))
            raw_seen = [Count() for _ in range(RAW)]
            jobs = [Count(), Count()]
            var_seen, rstd_seen, h_seen, rows_seen = (Count() for _ in range(4))

            def hi(width=CW):
                n = conv.base
                act.wait_ge(raw_loaded[n % RAW], raw_seen[n % RAW].add(16))
                if n >= RING:
                    act.wait_ge(w_used, conv.at(1 - RING))
                src = raw[:, n % RAW, :].rearrange("p (k c) -> p k c", k=2)[:, :, 0:width]
                dst = wh[:, n % RING, :].rearrange("p (k c) -> p k c", k=2)[:, :, 0:width]
                act.activation(dst, src, ACT.Copy).then_inc(w_hi_ready, 1)
                conv.add()

            def hi_steps(n=1):
                return {conv: 8 * n, half0: n, used: 8 * n, jobs[0]: n, jobs[1]: n,
                        **{raw_seen[i]: 32 * n for i in range(RAW)}}

            def job_done(t, pairs=8):
                if t == 0:
                    act.wait_ge(half0_done, half0.add())
                else:
                    act.wait_ge(w_used, used.add(pairs))
                jobs[t].add()

            def square(src, accum):
                if sq.base:
                    act.wait_ge(sq_done, sq.at())
                act.activation(ps[:, JUNK, 0:CW], src, ACT.Square, accum_out=accum).then_inc(sq_done, 1)
                sq.add()

            def root():
                act.wait_ge(var_ready, var_seen.add())
                act.activation(std, var, ACT.Sqrt).then_inc(std_ready, 1)

            def scaled_row(t, norm, width=CW):
                act.activation(row[:, t, 0:width], ps[:, G[t], 0:width], ACT.Copy,
                               scale=rstd(norm, t)).then_inc(bank_free[t], 1)

            def split_hi(dst, t, gain=None):
                act.wait_ge(split_t_done, split_n.add())
                b = T[(split_n.base - 1) % 2]
                tok = slice(t * P, (t + 1) * P)
                if gain is None:
                    act.activation(dst[:, :, tok], ps[:, b, :].rearrange("p (k s) -> p k s", k=4), ACT.Copy)\
                       .then_inc(split_hi_done, 1)
                    return
                for i in range(4):
                    last = act.activation(dst[:, i, tok], ps[:, b, i * P:(i + 1) * P], ACT.Copy,
                                          scale=gt[:, gain + i:gain + i + 1])
                last.then_inc(split_hi_done, 1)

            def plain_copy(dst, t, blocks):
                act.wait_ge(plain_t_done, plain_n.add())
                b = L[(plain_n.base - 1) % 2]
                act.activation(dst[:, :, t * P:(t + 1) * P],
                               ps[:, b, 0:blocks * P].rearrange("p (k s) -> p k s", k=blocks), ACT.Copy)\
                   .then_inc(plain_copied, 1)

            act.wait_ge(tables_loaded, 64)
            for n in range(4):
                act.wait_ge(xt_loaded[n], 16)
                for kt in range(4 * n, 4 * n + 4):
                    act.activation(xh[:, kt, :], x_raw[:, kt, :], ACT.Copy, scale=gt[:, kt:kt + 1]).then_inc(x_hi, 1)
                hi()
            for n in range(4):
                hi()
            act.wait_ge(x_loaded, 16)
            for t in range(HALVES):
                for i in range(4):
                    square(h[:, t, i * CW:(i + 1) * CW], ssq(N_PRE0, t, i, i + 1))
            for t in range(HALVES):
                root()
            act.wait_ge(angles_ready, 1)
            act.activation(row[:, 0, 0:384], row[:, 0, 0:384], ACT.Sin).then_inc(sines_ready, 1)
            act.wait_ge(angles_ready, 2)
            act.wait_ge(rstd_ready, rstd_seen.add(2))

            for c in range(5):
                for t in range(HALVES):
                    nexts = (IN_WIDTHS + (Q_UP_W,))[c + 1]
                    job_done(t)
                    if c < 4:
                        scaled_row(t, N_PRE0)
                    else:
                        act.activation(row[:, t, 0:192], ps[:, G[t], 0:192], ACT.Copy, scale=rstd(N_PRE0, t))
                        act.activation(swa_v[:, t, :], ps[:, G[t], 192:320], ACT.Copy,
                                       scale=rstd(N_PRE0, t)).then_inc(bank_free[t], 1)
                    if c < 2:
                        act.wait_ge(bank_free[t], jobs[t].at())
                        square(row[:, t, :], ssq(N_Q + c, t, 0, 1))
                        root()
                    for _ in range(5 if t == 0 else 3):
                        hi(nexts)
                    if c < 2:
                        split_hi(al[:, 8 * c:8 * c + 4, :], t, gain=64 + 4 * c)
                    elif c < 4:
                        plain_copy(swa_q[:, 4 * c - 8:4 * c - 4, :], t, 4)
                    else:
                        plain_copy(swa_k, t, 3)

            act.wait_ge(rstd_ready, rstd_seen.add(4))
            for c in range(8):
                for t in range(HALVES):
                    job_done(t, 2)
                    if c < 4:
                        scaled_row(t, N_Q, Q_UP_W)
                    else:
                        act.activation(row[:, t, 0:256], ps[:, G[t], 0:256], ACT.Copy, scale=rstd(N_KV, t))
                        act.activation(vm[:, t, (c - 4) * 256:(c - 3) * 256], ps[:, G[t], 256:512], ACT.Copy,
                                       scale=rstd(N_KV, t)).then_inc(bank_free[t], 1)
                    if t == 1:
                        hi()
                        hi()
                    if c < 4:
                        plain_copy(mla_q[:, c, :, :], t, 3)
                    else:
                        plain_copy(mla_k[:, 2 * c - 8:2 * c - 6, :], t, 2)

            def exps(n, sink=None):
                act.wait_ge(nmax_ready, n + 1)
                for t, (a, b) in enumerate(((0, P), (P, 3 * P))):
                    last = act.activation(prob[n % 3][:, a:b], prob[n % 3][:, a:b], ACT.Exp,
                                          bias=nmax[n % 3][:, t:t + 1], accum_out=rsum[n % 3][:, t:t + 1])
                if sink is not None:
                    last = act.activation(esink[n % 3], nmax[n % 3], ACT.Exp, bias=sinkv[:, sink:sink + 1])
                last.then_inc(exp_done, 1)

            def copy_probs(n):
                act.wait_ge(pt_done, n + 1)
                if n >= 2:
                    act.wait_ge(o_done, n - 1)
                act.activation(prob_t[n % 2], ps[:, T[n % 2], 0:3 * P], ACT.Copy).then_inc(pt_copied, 1)

            def out_hi(n, kt, bank):
                act.wait_ge(o_done, n + 1)
                act.activation(xh[:, kt, :], ps[:, G[bank], 0:SEQ], ACT.Copy).then_inc(o_hi, 1)

            def attention(first, heads):
                for i in range(len(heads) + 2):
                    if i < len(heads):
                        exps(first + i, heads[i][0])
                    if i >= 2 and heads[i - 2][1] is not None:
                        out_hi(first + i - 2, heads[i - 2][1], heads[i - 2][1] % 2)
                    if 1 <= i <= len(heads):
                        copy_probs(first + i - 1)

            attention(0, [(None, hd) for hd in range(MLA_H)]
                      + [(hd, MLA_H + hd // 2 if hd % 2 else None) for hd in range(SWA_H)])

            def update_h(t, pre, hi_left):
                root()
                for n in range(hi_left):
                    hi()
                    if n == 0 and pre is not None:
                        for i in range(4):
                            act.wait_ge(h_ready, h_seen.add())
                            square(h[:, t, i * CW:(i + 1) * CW], ssq(pre, t, i, i + 1))
                if pre is None:
                    h_seen.add(4)

            def split_h(t, pre, gain, dst, hi_left):
                for i in range(4):
                    split_hi(dst[:, 4 * i:4 * i + 4, :], t, None if gain is None else gain + 4 * i)
                    if i < hi_left:
                        hi()
                if pre is not None:
                    root()

            def block_rest(layer):
                post, mpre, mpost = ((N_POST0, N_MPRE0, N_MPOST0), (N_POST1, N_MPRE1, N_MPOST1))[layer]
                last_layer = layer == 1

                def out_chunk(i, last):
                    for t in range(HALVES):
                        job_done(t)
                        square(ps[:, G[t], :], stats[:, bass.ds(i + (10 * post + 5 * t), 1)])
                        todo = 5 if t == 0 else 3
                        if last:
                            update_h(t, mpre, todo - 2)
                            split_h(t, mpre, 16 * (2 + layer), xh, 2)
                        else:
                            for _ in range(todo):
                                hi()

                with repeat(act, 3, {**hi_steps(), sq: 2}) as i:
                    out_chunk(i, False)
                out_chunk(3, True)

                act.wait_ge(rstd_ready, rstd_seen.add(4))

                def up(i):
                    for t in range(HALVES):
                        job_done(t)
                        act.activation(row[:, t, :], ps[:, G[t], :], ACT.Relu, scale=rstd(mpre, t))\
                           .then_inc(bank_free[t], 1)
                        hi()
                        hi()
                        split_hi(ah[:, bass.ds(i * 4, 4), :], t)
                        for _ in range(3 if t == 0 else 1):
                            hi()

                def ups():
                    with repeat(act, 4, {**hi_steps(), split_n: 2}) as i:
                        up(i)

                with repeat(act, 3, {**hi_steps(8), split_n: 8}):
                    ups()
                    with repeat(act, 4, hi_steps()):
                        for t in range(HALVES):
                            job_done(t)
                            for _ in range(5 if t == 0 else 3):
                                hi()
                ups()
                act.wait_ge(p_loaded, 16 * layer + 16)
                act.activation(xh[:, 0:2, :], p_raw, ACT.Copy).then_inc(p_hi, 1)

                def last_down(i, last):
                    for t in range(HALVES):
                        job_done(t)
                        act.wait_ge(bank_free[t], jobs[t].at())
                        square(m[:, t, bass.ds(i * CW, CW)], stats[:, bass.ds(i + (10 * mpost + 5 * t), 1)])
                        if not last:
                            for _ in range(5 if t == 0 else 3):
                                hi()
                        elif t == 0:
                            hi()
                            update_h(t, None, 2)
                            split_h(t, None, None, ah, 2)
                        else:
                            hi()
                            update_h(t, None, 2)

                with repeat(act, 3, {**hi_steps(), sq: 2}) as i:
                    last_down(i, False)
                last_down(3, True)

                for c in range(CHUNKS):
                    for t in range(HALVES):
                        job_done(t, 1)
                        dst = m[:, 0, :] if t == 0 else proj1
                        act.activation(dst[:, c * CW:(c + 1) * CW], ps[:, G[t], :], ACT.Copy).then_inc(bank_free[t], 1)
                    hi()
                split_h(1, None, None, ah, 0)

                def gate(i, convert=True):
                    for t in range(HALVES):
                        job_done(t)
                        act.wait_ge(bank_free[t], jobs[t].at())
                        act.activation(row[:, t, :], row[:, t, :], ACT.Sigmoid).then_inc(sig_done, 1)
                        todo = (5 if t == 0 else 3) if convert else 0
                        for _ in range(min(todo, 2)):
                            hi()
                        act_rows = rows_seen.add()
                        if not last_layer:
                            act.wait_ge(row_done, act_rows)
                            act.activation(h[:, t, bass.ds(i * CW, CW)], row[:, t, :], ACT.Copy).then_inc(h_saved, 1)
                            square(row[:, t, :], stats[:, bass.ds(i + (10 * N_PRE1 + 5 * t), 1)])
                        for _ in range(todo - min(todo, 2)):
                            hi()
                        if not last_layer:
                            act.wait_ge(split_t_done, split_n.add())
                            b = T[(split_n.base - 1) % 2]
                            tok = slice(t * P, (t + 1) * P)
                            for k in range(4):
                                last = act.activation(xh[:, bass.ds(i * 4 + k, 1), tok],
                                                      ps[:, b, k * P:(k + 1) * P].unsqueeze(1),
                                                      ACT.Copy, scale=gt[:, bass.ds(i * 4 + (16 + k), 1)])
                            last.then_inc(split_hi_done, 1)

                if not last_layer:
                    with repeat(act, 4, {**hi_steps(), sq: 2, split_n: 2, rows_seen: 2}) as i:
                        gate(i)
                    root()
                    root()
                    act.wait_ge(rstd_ready, rstd_seen.add(4))
                else:
                    with repeat(act, 3, {**hi_steps(), rows_seen: 2}) as i:
                        gate(i)
                    gate(3, False)

            rows_seen.add(ROWS_BEFORE_GATE[0])
            block_rest(0)

            with repeat(act, 8, {**hi_steps(), plain_n: 2}) as i:
                for t in range(HALVES):
                    job_done(t)
                    scaled_row(t, N_PRE1)
                    for _ in range(5 if t == 0 else 3):
                        hi()
                    plain_copy(moba_qk[:, bass.ds(i * 4, 4), :], t, 4)
            with repeat(act, 4, hi_steps()) as i:
                for t in range(HALVES):
                    job_done(t)
                    act.activation(m[:, t, bass.ds(i * CW, CW)], ps[:, G[t], :], ACT.Copy,
                                   scale=rstd(N_PRE1, t)).then_inc(bank_free[t], 1)
                    for _ in range(5 if t == 0 else 3):
                        hi()
            attention(MLA_H + SWA_H, [(None, hd) for hd in range(MOBA_H)])
            rows_seen.add(ROWS_BEFORE_GATE[1] - rows_seen.base)
            block_rest(1)
            assert conv.base == PAIRS

        @block.vector
        def _(dve):
            conv, half0, used, sq, split_n = (Count() for _ in range(5))
            jobs = [Count(), Count()]
            steps, roots, rows_out, h_out, sigs = (Count() for _ in range(5))

            def link(ins):
                ins.then_inc(dve_step, 1)
                dve.wait_ge(dve_step, steps.add())

            def lo(width=CW):
                n = conv.base
                dve.wait_ge(w_hi_ready, conv.add())
                k = lambda ap: ap.rearrange("p (k c) -> p k c", k=2)[:, :, 0:width]
                dve.tensor_tensor(k(wl[:, n % RING, :]), k(raw[:, n % RAW, :]), k(wh[:, n % RING, :].bitcast(F32)),
                                  ALU.subtract).then_inc(w_lo_ready, 1)

            def lo_steps(n=1):
                return {conv: 8 * n, half0: n, used: 8 * n, jobs[0]: n, jobs[1]: n}

            def job_done(t, pairs=8):
                if t == 0:
                    dve.wait_ge(half0_done, half0.add())
                else:
                    dve.wait_ge(w_used, used.add(pairs))
                jobs[t].add()

            def skip_job(t, pairs=8):
                if t == 0:
                    half0.add()
                else:
                    used.add(pairs)
                jobs[t].add()

            def variance(norm, t, n, dim):
                dve.wait_ge(sq_done, sq.at())
                src = ssq(norm, t, 0, 1)
                if n > 1:
                    link(dve.tensor_reduce(var, ssq(norm, t, 0, n), AX, ALU.add))
                    src = var
                dve.tensor_scalar(var, src, 1.0 / dim, EPS, ALU.mult, ALU.add).then_inc(var_ready, 1)
                roots.add()

            def inverse_root(norm, t):
                dve.wait_ge(std_ready, roots.at())
                link(dve.reciprocal(rec, std))
                link(dve.scalar_tensor_tensor(cor, rec, rec, var, ALU.mult, ALU.mult))
                link(dve.tensor_scalar(cor, cor, -0.5, 1.5, ALU.mult, ALU.add))
                dve.tensor_tensor(rstd(norm, t), cor, rec, ALU.mult).then_inc(rstd_ready, 1)
                dve.wait_ge(rstd_ready, roots.at())

            def split_lo(dst, dst_hi, t, gain=None):
                dve.wait_ge(split_hi_done, split_n.add())
                b = T[(split_n.base - 1) % 2]
                tok = slice(t * P, (t + 1) * P)
                if gain is None:
                    dve.tensor_tensor(dst[:, :, tok], ps[:, b, :].rearrange("p (k s) -> p k s", k=4),
                                      dst_hi[:, :, tok].bitcast(F32), ALU.subtract).then_inc(split_lo_done, 1)
                    return
                for i in range(4):
                    last = dve.scalar_tensor_tensor(dst[:, i, tok], ps[:, b, i * P:(i + 1) * P],
                                                    gt[:, gain + i:gain + i + 1], dst_hi[:, i, tok].bitcast(F32),
                                                    ALU.mult, ALU.subtract)
                last.then_inc(split_lo_done, 1)

            def rope(t, a, n, half, cos, sin, dst=None):
                r = row[:, t, a:a + 2 * n * half].rearrange("p (n j d) -> p n j d", n=n, j=2)
                s = tmp[:, 0:2 * n * half].rearrange("p (n j d) -> p n j d", n=n, j=2)
                for j in range(2):
                    part = sin[:, t, j, :].unsqueeze(1).to_broadcast([P, n, half])
                    link(dve.tensor_tensor(s[:, :, j, :], r[:, :, 1 - j, :], part, ALU.mult))
                both = cos[:, t, :].unsqueeze(1).unsqueeze(1).to_broadcast([P, n, 2, half])
                link(dve.tensor_tensor(r, r, both, ALU.mult))
                if dst is None:
                    dve.tensor_tensor(r, r, s, ALU.add).then_inc(row_done, 1)
                else:
                    d = dst.rearrange("p (n two c) -> p n two c", n=n, two=2)
                    flat = lambda ap: ap.rearrange("p n j d -> p n (j d)")
                    link(dve.tensor_tensor(d[:, :, 0, :], flat(r), flat(s), ALU.add))
                    dve.tensor_tensor(d[:, :, 1, :], flat(r), flat(s), ALU.add).then_inc(row_done, 1)
                rows_out.add()
                dve.wait_ge(row_done, rows_out.at())

            dve.wait_ge(tables_loaded, 64)
            posf = stats[:, 120:122]
            ang, fold = row[:, 0, 0:192], row[:, 0, 192:384]
            turns_i, turns = row[:, 1, 0:192].bitcast(I32), row[:, 1, 192:384]
            link(dve.tensor_copy(posf, pos_i[:, :]))
            for t in range(HALVES):
                link(dve.tensor_scalar(ang[:, 96 * t:96 * t + 96], tmp[:, 0:96], posf[:, t:t + 1], None, ALU.mult))
            link(dve.tensor_scalar(turns_i, ang, 1.0 / TWO_PI, None, ALU.mult))
            link(dve.tensor_copy(turns, turns_i))
            for part in (PI_A, PI_B, PI_C):
                link(dve.scalar_tensor_tensor(ang, turns, -part, ang, ALU.mult, ALU.add))
            link(dve.tensor_scalar(ang, ang, PI_MAX, -PI_MAX, ALU.min, ALU.max))
            link(dve.scalar_tensor_tensor(fold, ang, -1.0, ang, ALU.mult, ALU.max))
            dve.tensor_scalar(fold, fold, -1.0, float(np.pi / 2), ALU.mult, ALU.add).then_inc(angles_ready, 1)
            link(dve.tensor_scalar(nsink[:, 0:SWA_H], sinkv, -1.0, None, ALU.mult))

            for n in range(4):
                for kt in range(4 * n, 4 * n + 4):
                    dve.wait_ge(x_hi, kt + 1)
                    dve.scalar_tensor_tensor(xl[:, kt, :], x_raw[:, kt, :], gt[:, kt:kt + 1],
                                             xh[:, kt, :].bitcast(F32), ALU.mult, ALU.subtract).then_inc(x_lo, 1)
                lo()
            for n in range(4):
                lo()
            sq.add(8)
            for t in range(HALVES):
                variance(N_PRE0, t, 4, D)
                inverse_root(N_PRE0, t)
            dve.wait_ge(sines_ready, 1)
            s3 = ang.rearrange("p (t f) -> p t f", t=2)
            c3 = fold.rearrange("p (t f) -> p t f", t=2)
            dve.tensor_copy(cos128[:, :, :], c3[:, :, 0:64])
            dve.tensor_copy(cos64[:, :, :], c3[:, :, 64:96])
            dve.tensor_copy(sin128[:, :, 1, :], s3[:, :, 0:64])
            dve.tensor_copy(sin64[:, :, 1, :], s3[:, :, 64:96])
            dve.tensor_scalar(sin128[:, :, 0, :], s3[:, :, 0:64], -1.0, None, ALU.mult)
            dve.tensor_scalar(sin64[:, :, 0, :], s3[:, :, 64:96], -1.0, None, ALU.mult).then_inc(angles_ready, 1)
            dve.wait_ge(angles_ready, 2)

            for c in range(5):
                for t in range(HALVES):
                    nexts = (IN_WIDTHS + (Q_UP_W,))[c + 1]
                    skip_job(t)
                    if c < 2:
                        sq.add()
                        variance(N_Q + c, t, 1, RANK)
                        inverse_root(N_Q + c, t)
                    else:
                        dve.wait_ge(bank_free[t], jobs[t].at())
                        if c < 4:
                            rope(t, 0, 8, 32, cos64, sin64)
                        else:
                            rope(t, 0, 3, 32, cos64, sin64, doubled[t])
                    for _ in range(5 if t == 0 else 3):
                        lo(nexts)
                    if c < 2:
                        split_lo(al[:, 8 * c + 4:8 * c + 8, :], al[:, 8 * c:8 * c + 4, :], t, gain=64 + 4 * c)

            for c in range(8):
                for t in range(HALVES):
                    skip_job(t, 2)
                    if c < 4:
                        dve.wait_ge(bank_free[t], jobs[t].at())
                        rope(t, 2 * NOPE, 2, 32, cos64, sin64)
                    if t == 1:
                        lo()
                        lo()

            def mask_scores(n, scale, mask, sink=None):
                p = prob[n % 3]
                dve.wait_ge(s_done, n + 1)
                if n >= 3:
                    dve.wait_ge(pt_done, n - 2)
                dve.scalar_tensor_tensor(p, ps[:, L[n % 2], 0:3 * P], scale, mask[:, :], ALU.mult, ALU.add)\
                   .then_inc(s_masked, 1)
                dve.wait_ge(s_masked, n + 1)
                link(dve.tensor_reduce(nmax[n % 3][:, 0:1], p[:, 0:P], AX, ALU.max, negate=True))
                last = dve.tensor_reduce(nmax[n % 3][:, 1:2], p[:, P:3 * P], AX, ALU.max, negate=True)
                if sink is not None:
                    link(last)
                    last = dve.tensor_scalar(nmax[n % 3], nmax[n % 3], nsink[:, sink:sink + 1], None, ALU.min)
                last.then_inc(nmax_ready, 1)

            def normalize(n, sink=False):
                p = prob[n % 3]
                dve.wait_ge(exp_done, n + 1)
                if sink:
                    link(dve.tensor_tensor(rsum[n % 3], rsum[n % 3], esink[n % 3], ALU.add))
                link(dve.reciprocal(rinv[n % 3], rsum[n % 3]))
                dve.tensor_scalar(p[:, 0:P], p[:, 0:P], rinv[n % 3][:, 0:1], None, ALU.mult)
                dve.tensor_scalar(p[:, P:3 * P], p[:, P:3 * P], rinv[n % 3][:, 1:2], None, ALU.mult).then_inc(p_ready, 1)

            splits = Count()

            def out_lo(kt, bank):
                dve.wait_ge(o_hi, splits.add())
                dve.tensor_tensor(xl[:, kt, :], ps[:, G[bank], 0:SEQ], xh[:, kt, :].bitcast(F32),
                                  ALU.subtract).then_inc(o_lo, 1)

            def attention(first, heads):
                for i in range(len(heads) + 2):
                    if i < len(heads):
                        mask_scores(first + i, *heads[i][0:3])
                    if i >= 2 and heads[i - 2][3] is not None:
                        out_lo(heads[i - 2][3], heads[i - 2][3] % 2)
                    if 1 <= i <= len(heads):
                        normalize(first + i - 1, heads[i - 1][2] is not None)

            dve.wait_ge(consts_ready, 6)
            attention(0, [((NOPE + ROPE) ** -0.5, mask_causal, None, hd) for hd in range(MLA_H)]
                      + [(SWA_D ** -0.5, mask_window, hd, MLA_H + hd // 2 if hd % 2 else None)
                         for hd in range(SWA_H)])

            def update_h(t, post, lo_left):
                variance(post, t, 4, D)
                inverse_root(post, t)
                for i in range(4):
                    cols = slice(i * CW, (i + 1) * CW)
                    dve.scalar_tensor_tensor(h[:, t, cols], m[:, t, cols], rstd(post, t), h[:, t, cols],
                                             ALU.mult, ALU.add).then_inc(h_ready, 1)
                h_out.add(4)
                for _ in range(lo_left):
                    lo()

            def split_h(t, pre, gain, dst_hi, dst_lo, lo_left):
                for i in range(4):
                    split_lo(dst_lo[:, 4 * i:4 * i + 4, :], dst_hi[:, 4 * i:4 * i + 4, :], t,
                             None if gain is None else gain + 4 * i)
                    if i < lo_left:
                        lo()
                if pre is not None:
                    sq.add(4)
                    variance(pre, t, 4, D)
                    inverse_root(pre, t)

            def block_rest(layer):
                post, mpre, mpost = ((N_POST0, N_MPRE0, N_MPOST0), (N_POST1, N_MPRE1, N_MPOST1))[layer]
                last_layer = layer == 1

                dve.wait_ge(row_bc_loaded, 16 * (3 * layer + 1))

                def out_chunk(i, last):
                    for t in range(HALVES):
                        skip_job(t)
                        sq.add()
                        dve.wait_ge(sq_done, sq.at())
                        cols = bass.ds(i * CW, CW)
                        dve.tensor_tensor(m[:, t, cols], ps[:, G[t], :], gbc[:, cols], ALU.mult)\
                           .then_inc(bank_free[t], 1)
                        todo = 5 if t == 0 else 3
                        if last:
                            dve.wait_ge(bank_free[t], jobs[t].at())
                            update_h(t, post, todo - 2)
                            split_h(t, mpre, 16 * (2 + layer), xh, xl, 2)
                        else:
                            for _ in range(todo):
                                lo()

                with repeat(dve, 3, {**lo_steps(), sq: 2}) as i:
                    out_chunk(i, False)
                out_chunk(3, True)

                def ups():
                    with repeat(dve, 4, {**lo_steps(), split_n: 2, rows_out: 2}) as i:
                        for t in range(HALVES):
                            skip_job(t)
                            dve.wait_ge(bank_free[t], jobs[t].at())
                            dve.tensor_tensor(row[:, t, :], row[:, t, :], row[:, t, :], ALU.mult).then_inc(row_done, 1)
                            rows_out.add()
                            lo()
                            lo()
                            split_lo(al[:, bass.ds(i * 4, 4), :], ah[:, bass.ds(i * 4, 4), :], t)
                            for _ in range(3 if t == 0 else 1):
                                lo()

                def add_down(i, t):
                    dve.wait_ge(bank_free[t], jobs[t].at())
                    job_done(t)
                    cols = bass.ds(i * CW, CW)
                    dve.tensor_tensor(m[:, t, cols], ps[:, G[t], :], m[:, t, cols], ALU.add).then_inc(bank_free[t], 1)

                dve.wait_ge(m_zeroed, layer + 1)
                with repeat(dve, 3, {**lo_steps(8), split_n: 8, rows_out: 8}):
                    ups()
                    with repeat(dve, 4, lo_steps()) as i:
                        for t in range(HALVES):
                            add_down(i, t)
                            for _ in range(5 if t == 0 else 3):
                                lo()
                ups()
                dve.wait_ge(p_hi, layer + 1)
                dve.tensor_tensor(xl[:, 0:2, :], p_raw, xh[:, 0:2, :].bitcast(F32), ALU.subtract).then_inc(p_lo, 1)
                dve.wait_ge(row_bc_loaded, 16 * (3 * layer + 2))

                def last_down(i, last):
                    for t in range(HALVES):
                        add_down(i, t)
                        todo = 4 if t == 0 else 2
                        lo()
                        sq.add()
                        dve.wait_ge(sq_done, sq.at())
                        cols = bass.ds(i * CW, CW)
                        link(dve.tensor_tensor(m[:, t, cols], m[:, t, cols], gbc[:, cols], ALU.mult))
                        if not last:
                            for _ in range(todo):
                                lo()
                        elif t == 0:
                            update_h(t, mpost, 2)
                            split_h(t, None, None, ah, al, 2)
                        else:
                            update_h(t, mpost, 2)

                with repeat(dve, 3, {**lo_steps(), sq: 2, steps: 2}) as i:
                    last_down(i, False)
                last_down(3, True)

                for c in range(CHUNKS):
                    for t in range(HALVES):
                        skip_job(t, 1)
                    lo()
                split_h(1, None, None, ah, al, 0)
                dve.wait_ge(h_ready, h_out.at())

                dve.wait_ge(row_bc_loaded, 16 * (3 * layer + 3))
                for t in range(HALVES):
                    dve.wait_ge(bank_free[t], jobs[t].at())

                stored = Count()

                def gate(i, convert=True, first=False):
                    for t in range(HALVES):
                        cols = bass.ds(i * CW, CW)
                        job_done(t)
                        if last_layer and not first:
                            dve.wait_ge(out_stored[t], stored.at(16))
                        dve.tensor_tensor(row[:, t, :], ps[:, G[t], :], gbc[:, cols], ALU.add).then_inc(bank_free[t], 1)
                        todo = (5 if t == 0 else 3) if convert else 0
                        if todo:
                            lo()
                        sigs.add()
                        dve.wait_ge(sig_done, sigs.at())
                        proj = m[:, 0, cols] if t == 0 else proj1[:, cols]
                        link(dve.tensor_tensor(row[:, t, :], row[:, t, :], proj, ALU.mult))
                        dve.tensor_tensor(row[:, t, :], row[:, t, :], h[:, t, cols], ALU.add).then_inc(row_done, 1)
                        rows_out.add()
                        for _ in range(todo - 1):
                            lo()
                        if not last_layer:
                            sq.add()
                            dve.wait_ge(split_hi_done, split_n.add())
                            b = T[(split_n.base - 1) % 2]
                            tok = slice(t * P, (t + 1) * P)
                            for k in range(4):
                                kt = bass.ds(i * 4 + k, 1)
                                last = dve.scalar_tensor_tensor(
                                    xl[:, kt, tok], ps[:, b, k * P:(k + 1) * P].unsqueeze(1),
                                    gt[:, bass.ds(i * 4 + (16 + k), 1)], xh[:, kt, tok].bitcast(F32),
                                    ALU.mult, ALU.subtract)
                            last.then_inc(split_lo_done, 1)
                    if last_layer and not first:
                        stored.add(16)

                if not last_layer:
                    with repeat(dve, 4, {**lo_steps(), sq: 2, split_n: 2, rows_out: 2, steps: 2, sigs: 2}) as i:
                        gate(i)
                    for t in range(HALVES):
                        variance(N_PRE1, t, 4, D)
                        inverse_root(N_PRE1, t)
                else:
                    gate(0, first=True)
                    with repeat(dve, 2, {**lo_steps(), rows_out: 2, steps: 2, sigs: 2, stored: 16}) as i:
                        gate(i + 1)
                    gate(3, convert=False)

            block_rest(0)

            with repeat(dve, 8, {**lo_steps(), rows_out: 2, steps: 6}):
                for t in range(HALVES):
                    skip_job(t)
                    dve.wait_ge(bank_free[t], jobs[t].at())
                    rope(t, 0, 4, 64, cos128, sin128)
                    for _ in range(5 if t == 0 else 3):
                        lo()
            with repeat(dve, 4, lo_steps()):
                for t in range(HALVES):
                    skip_job(t)
                    for _ in range(5 if t == 0 else 3):
                        lo()
            attention(MLA_H + SWA_H, [(MOBA_D ** -0.5, mask_causal, None, hd) for hd in range(MOBA_H)])
            block_rest(1)
            assert conv.base == PAIRS


_OUT = (1, SEQ, D)


def _pairs(w):
    k, n = w.shape
    return w.reshape(k // 256, 2, P, n // CW, CW).transpose(3, 0, 2, 1, 4).reshape(-1, P, 2 * CW)


def _padded(w):
    full = np.zeros((w.shape[0], CW), w.dtype)
    full[:, :w.shape[1]] = w
    return _pairs(full)


def _mlp_pairs(up, down):
    parts = []
    for g in range(GROUPS):
        parts += [_pairs(up[:, g * D:(g + 1) * D]), _pairs(down[g * D:(g + 1) * D, :])]
    return parts


def _stream(w_in, q_up, kv_up, even_out, qkv, odd_out, mlp_up, mlp_down, ple_proj, ple_gate):
    o_kr = 2 * RANK
    o_qs = o_kr + ROPE
    o_ks = o_qs + SWA_H * SWA_D
    o_vs = o_ks + SWA_KV * SWA_D
    parts = [_pairs(w_in[:, 0:2 * RANK]), _pairs(w_in[:, o_qs:o_ks]),
             _padded(np.concatenate([w_in[:, o_ks:o_vs], w_in[:, o_kr:o_qs], w_in[:, o_vs:]], axis=1))]
    q = q_up.reshape(RANK, MLA_H, NOPE + ROPE)
    for c in range(MLA_H // 2):
        a, b = 2 * c, 2 * c + 1
        parts.append(_padded(np.concatenate([q[:, a, :NOPE], q[:, b, :NOPE], q[:, a, NOPE:], q[:, b, NOPE:]], axis=1)))
    kv = kv_up.reshape(RANK, MLA_H, 2, 128)
    for c in range(MLA_H // 2):
        a, b = 2 * c, 2 * c + 1
        parts.append(_pairs(np.concatenate([kv[:, a, 0], kv[:, b, 0], kv[:, a, 1], kv[:, b, 1]], axis=1)))
    parts.append(_pairs(even_out))
    parts += _mlp_pairs(mlp_up[0], mlp_down[0]) + [_pairs(ple_proj[0]), _pairs(ple_gate[0])]
    parts += [_pairs(qkv), _pairs(odd_out)]
    parts += _mlp_pairs(mlp_up[1], mlp_down[1]) + [_pairs(ple_proj[1]), _pairs(ple_gate[1])]
    return np.concatenate(parts)


def _by_k(v):
    return v.reshape(-1, P).T


def kernel(x, p, positions, even_pre_g, even_w_in, mla_q_norm_g, mla_w_q_up, mla_kv_norm_g, mla_w_kv_up,
           swa_sinks, even_w_out, even_post_g, odd_pre_g, moba_w_qkv, odd_w_out, odd_post_g, mlp_pre_g,
           mlp_w_up, mlp_w_down, mlp_post_g, ple_w_gate, ple_b_gate, ple_w_proj):
    import concourse.bacc as bacc
    from concourse.bass_utils import run_bass_kernel_spmd

    a = lambda v: np.asarray(v)
    x2 = a(x)[0]
    half = np.arange(64, dtype=np.float64)
    arrays = {
        "x": x2,
        "x_t": x2.T.reshape(KT, P, SEQ).transpose(1, 0, 2),
        "p_t": a(p)[:, 0].transpose(0, 2, 1).reshape(2, 2, P, SEQ).transpose(0, 2, 1, 3),
        "pos": a(positions)[0].reshape(HALVES, P).T,
        "gains_t": np.concatenate([_by_k(a(g)) for g in (even_pre_g[0], odd_pre_g[0], mlp_pre_g[0], mlp_pre_g[1],
                                                         mla_q_norm_g[0], mla_kv_norm_g[0])], axis=1),
        "rows": np.stack([a(g) for g in (even_post_g[0], mlp_post_g[0], ple_b_gate[0],
                                         odd_post_g[0], mlp_post_g[1], ple_b_gate[1])]),
        "sinks": a(swa_sinks)[0],
        "freqs": np.concatenate([THETA ** (-half * (2.0 / MOBA_D)), THETA ** (-half[:32] * (2.0 / ROPE))])
                   .astype(np.float32),
        "w_stream": _stream(a(even_w_in)[0], a(mla_w_q_up)[0], a(mla_w_kv_up)[0], a(even_w_out)[0],
                            a(moba_w_qkv)[0], a(odd_w_out)[0], a(mlp_w_up), a(mlp_w_down),
                            a(ple_w_proj), a(ple_w_gate)),
    }
    arrays = {f"in_{n}": np.ascontiguousarray(v) for n, v in arrays.items()}
    nc = bacc.Bacc("TRN2", target_bir_lowering=False, num_devices=1)
    args = [nc.dram_tensor(n, v.shape, mybir.dt.from_np(v.dtype), kind="ExternalInput").ap()
            for n, v in arrays.items()]
    out = nc.dram_tensor("out", (SEQ, D), F32, kind="ExternalOutput").ap()
    build(nc, *args, out)
    r = run_bass_kernel_spmd(nc, [arrays], core_ids=[0])
    return r.results[0]["out"].reshape(_OUT)
```

```python
from contextlib import ExitStack, contextmanager

import numpy as np
import concourse.bass as bass
from concourse import mybir

ALU = mybir.AluOpType
ACT = mybir.ActivationFunctionType
AX = mybir.AxisListType.X
F32 = mybir.dt.float32
F32R = mybir.dt.float32r
I32 = mybir.dt.int32

P = 128
HALVES = 2
SEQ = P * HALVES
D = 2048
KT = D // P
CW = 512
CHUNKS = D // CW
DFF = 4 * D
GROUPS = DFF // D
EPS = 1e-6
THETA = 10000.0
RAW = 4
RING = 8
PROBS = 4
EARLY = 4
OUT_PAIRS = ((1, 1, 1, 1), (1, 1, 0, 0))
DOWN_PAIRS = (1, 1, 1, 1)
ODD_START = ((3, 0), (1, 1))
MLA_H, NOPE, ROPE, RANK = 8, 128, 64, 512
SWA_H, SWA_KV, SWA_D = 16, 2, 64
MOBA_H, MOBA_D = 16, 128
PLE = 256
NEG = -3.0e38
TWO_PI = 2.0 * np.pi
PI_A = 6.28125
PI_B = float(np.float32(np.float32((TWO_PI - PI_A) * 2**21).round() / 2**21))
PI_C = float(TWO_PI - PI_A - PI_B)
PI_MAX = 3.1415925

IN_WIDTHS = (512, 512, 512, 512, 320)
Q_UP_W = 2 * (NOPE + ROPE)
PAIRS = (5 * 8 + 4 * 2 + 4 * 2 + 4 * 8 + GROUPS * 8 * 8 + 4 + 4 * 8
         + 12 * 8 + 4 * 8 + GROUPS * 8 * 8 + 4 + 4 * 8)
ROWS_BEFORE_GATE = (3 * 2 + 4 * 2 + GROUPS * 4 * 2, 3 * 2 + 4 * 2 + GROUPS * 4 * 2 + 8 + 8 * 2 + GROUPS * 4 * 2)


class Count:

    def __init__(self, base=0):
        self.base, self.terms = base, []

    def add(self, n=1):
        self.base += n
        return self.at()

    def at(self, plus=0):
        value = self.base + plus
        for reg, step in self.terms:
            value = reg * step + value
        return value


@contextmanager
def repeat(eng, times, steps):
    with eng.Fori(0, times) as i:
        before = {c: c.base for c in steps}
        for c, step in steps.items():
            c.terms.append((i, step))
        yield i
        for c, step in steps.items():
            assert c.base - before[c] == step, (c.base - before[c], step)
            c.terms.pop()
    for c, step in steps.items():
        c.base += (times - 1) * step


def build(nc, x, x_t, p_t, pos, gains_t, rows, sinks, freqs, w_stream, out):
    ctx = ExitStack()
    with ctx:
        def sb(name, shape, dt=F32):
            return ctx.enter_context(nc.sbuf_tensor(name, shape, dt))

        def sem(name):
            return ctx.enter_context(nc.semaphore(name))

        with nc.sbuf_tensor("mla_q_swa_kv", [P, 4096], F32) as over_m, \
                nc.sbuf_tensor("mla_k_swa_q", [P, 4096], F32) as over_a:
            pass
        with nc.sbuf_tensor("spacer", [P, 4096], F32), \
                nc.sbuf_tensor("moba_qk", [P, 8192], F32) as over_qk:
            pass
        m = sb("mixed", [P, HALVES, D])
        ah = sb("hidden_hi", [P, KT, SEQ], F32R)
        al = sb("hidden_lo", [P, KT, SEQ], F32R)
        xh = sb("act_hi", [P, KT, SEQ], F32R)
        xl = sb("act_lo", [P, KT, SEQ], F32R)
        h = sb("residual", [P, HALVES, D])
        raw = sb("w_raw", [P, RAW, 2 * CW])
        wh = sb("w_hi", [P, RING, 2 * CW], F32R)
        wl = sb("w_lo", [P, RING, 2 * CW], F32R)
        vm = sb("mla_v_ple", [P, HALVES, MLA_H * 128])
        gbc = sb("row_bc", [P, D])
        row = sb("row", [P, HALVES, CW])
        tmp = sb("tmp", [P, CW])
        ident = sb("ident", [P, P])
        ones = sb("ones", [P, 1])
        warm = sb("warm", [P, 1])
        mask_causal = sb("mask_causal", [P, 3 * P])
        mask_window = sb("mask_window", [P, 3 * P])
        cos64 = sb("cos64", [P, HALVES, 32])
        sin64 = sb("sin64", [P, HALVES, 2, 32])
        cos128 = sb("cos128", [P, HALVES, 64])
        sin128 = sb("sin128", [P, HALVES, 2, 64])
        gt = sb("gains_k", [P, 72])
        stats = sb("stats", [P, 128])
        nsink = sb("neg_sinks", [P, 2 * SWA_H])
        pos_i = sb("pos_i", [P, HALVES], I32)
        ps = ctx.enter_context(nc.psum_tensor("banks", [P, 8, CW], F32))
        G, T, L, JUNK = (0, 1), (2, 3), (4, 5), 7
        X_SUM = (6, JUNK)
        S = (6, JUNK, 4)
        O = (5, 1)

        mla_q = over_m[:, 0:3072].rearrange("p (c b t) -> p c b t", c=4, b=3)
        swa_k = over_m[:, 3072:3840].rearrange("p (b t) -> p b t", b=3)
        swa_v = over_m[:, 3840:4096].rearrange("p (t c) -> p t c", t=2)
        mla_k = over_a[:, 0:2048].rearrange("p (b t) -> p b t", b=8)
        swa_q = over_a[:, 2048:4096].rearrange("p (b t) -> p b t", b=8)
        moba_qk = over_qk[:, :].rearrange("p (b t) -> p b t", b=32)
        x_sq = over_a[:, :].rearrange("p (k s) -> p k s", s=SEQ)
        x_raw = m[:, :, :].rearrange("p t (k s) -> p (t k) s", s=SEQ)
        p_raw = tmp[:, :].rearrange("p (k s) -> p k s", k=2)
        proj1 = vm[:, :, :].rearrange("p t c -> p (t c)")
        prob = [gbc[:, 384 * i:384 * i + 384] for i in range(PROBS)]
        prob_t = [row[:, i, 0:384] for i in range(2)]
        doubled = [gbc[:, 384 * t:384 * t + 384] for t in range(HALVES)]
        sinkv = nsink[:, SWA_H:2 * SWA_H]

        angles = gbc[:, 0:384]
        x_part = gbc[:, D // 2:D].rearrange("p (n s) -> p n s", n=4)

        def ssq(norm, t, a=0, b=4):
            return stats[:, 10 * norm + 5 * t + a:10 * norm + 5 * t + b]

        def rstd(norm, t):
            return stats[:, 10 * norm + 5 * t + 4:10 * norm + 5 * t + 5]

        N_PRE0, N_Q, N_KV, N_POST0, N_MPRE0, N_MPOST0, N_PRE1, N_POST1, N_MPRE1, N_MPOST1 = range(10)
        var, std, rec, cor = (stats[:, 100 + i:101 + i] for i in range(4))
        nmax = [stats[:, 104 + 2 * i:106 + 2 * i] for i in range(3)]
        rsum = [stats[:, 110 + 2 * i:112 + 2 * i] for i in range(3)]
        esink = [stats[:, 116 + 2 * i:118 + 2 * i] for i in range(3)]
        rinv = [stats[:, 122 + 2 * i:124 + 2 * i] for i in range(3)]

        raw_loaded = [sem(f"raw_loaded{i}") for i in range(RAW)]
        gains_loaded, tables_loaded = sem("gains_loaded"), sem("tables_loaded")
        x_loaded, p_loaded = sem("x_loaded"), sem("p_loaded")
        xt_loaded = {kt: sem(f"xt_loaded{kt}") for kt in (0, 2, 4, 8, 12)}
        row_bc_loaded = sem("row_bc_loaded")
        out_stored = [sem(f"out_stored{t}") for t in range(HALVES)]
        last_stored = [sem(f"last_stored{t}") for t in range(HALVES)]
        w_hi_ready, w_lo_ready = sem("w_hi_ready"), sem("w_lo_ready")
        w_used = sem("w_used")
        half0_done = sem("half0_done")
        bank_free = [sem(f"bank_free{t}") for t in range(HALVES)]
        row_done = sem("row_done")
        sq_done = sem("sq_done")
        h_ready = sem("h_ready")
        h_saved = sem("h_saved")
        split_t_done = sem("split_t_done")
        split_hi_done, split_lo_done = sem("split_hi_done"), sem("split_lo_done")
        plain_t_done, plain_copied = sem("plain_t_done"), sem("plain_copied")
        var_ready, std_ready, rstd_ready = sem("var_ready"), sem("std_ready"), sem("rstd_ready")
        consts_ready = sem("consts_ready")
        angles_ready, sines_ready = sem("angles_ready"), sem("sines_ready")
        x_squared, x_partial, x_summed = sem("x_squared"), sem("x_partial"), sem("x_summed")
        x_hi, x_lo, p_hi, p_lo = sem("x_hi"), sem("x_lo"), sem("p_hi"), sem("p_lo")
        m_zeroed = sem("m_zeroed")
        sig_done = sem("sig_done")
        s_done, s_masked, nmax_ready = sem("s_done"), sem("s_masked"), sem("nmax_ready")
        exp_done, p_ready = sem("exp_done"), sem("p_ready")
        pt_done, pt_copied, o_done = sem("pt_done"), sem("pt_copied"), sem("o_done")
        o_hi, o_lo = sem("o_hi"), sem("o_lo")
        dve_step, pool_step = sem("dve_step"), sem("pool_step")

        block = ctx.enter_context(nc.Block())

        @block.sync
        def _(sp):
            sp.dma_start(gt[:], gains_t).then_inc(gains_loaded, 16)
            for n in range(2 * RAW):
                if n >= RAW:
                    sp.wait_ge(w_lo_ready, n + 1 - RAW)
                sp.dma_start(raw[:, n % RAW, :], w_stream[n]).then_inc(raw_loaded[n % RAW], 16)
                parts = (slice(0, 2), slice(2, 4)) if n == 0 else (slice(2 * n, 2 * n + 4),) if n % 2 == 0 else ()
                for part in parts:
                    sp.dma_start(x_raw[:, part, :], x_t[:, part, :]).then_inc(xt_loaded[part.start], 16)
                if n == RAW - 1:
                    sp.dma_start(pos_i[:], pos).then_inc(tables_loaded, 16)
                    sp.dma_start(tmp[:, 0:96], freqs.partition_broadcast(P)).then_inc(tables_loaded, 16)
                    sp.dma_start(sinkv, sinks.partition_broadcast(P)).then_inc(tables_loaded, 16)
            with sp.Fori(2, 4) as i:
                for n in range(RAW):
                    sp.wait_ge(w_lo_ready, i * RAW + (n - RAW + 1))
                    sp.dma_start(raw[:, n, :], w_stream[i * RAW + n]).then_inc(raw_loaded[n], 16)
            sp.dma_start(h[:, :, :], x.rearrange("(t p) d -> p t d", p=P)).then_inc(x_loaded, 16)
            with sp.Fori(4, PAIRS // RAW) as i:
                for n in range(RAW):
                    sp.wait_ge(w_lo_ready, i * RAW + (n - RAW + 1))
                    sp.dma_start(raw[:, n, :], w_stream[i * RAW + n]).then_inc(raw_loaded[n], 16)
            for t in range(HALVES):
                sp.wait_ge(row_done, ROWS_BEFORE_GATE[1] + HALVES * (CHUNKS - 1) + t + 1)
                sp.dma_start(out[t * P:(t + 1) * P, D - CW:D], row[:, t, :]).then_inc(last_stored[t], 16)
            for t in range(HALVES):
                sp.wait_ge(last_stored[t], 16)

        @block.gpsimd
        def _(pool):
            steps = Count()

            def link(ins):
                ins.then_inc(pool_step, 1)
                pool.wait_ge(pool_step, steps.add())

            pool.memset(ones[:, :], 1.0).then_inc(consts_ready, 1)
            link(pool.memset(ident[:, :], 0.0))
            pool.affine_select(out=ident[:, :], in_=ident[:, :], compare_op=ALU.not_equal, fill=1.0,
                               base=0, pattern=[[-1, P]], channel_multiplier=1).then_inc(consts_ready, 1)
            link(pool.memset(mask_causal[:, :], 0.0))
            link(pool.memset(mask_window[:, :], 0.0))
            for k, mask in enumerate((mask_causal, mask_causal, mask_window, mask_window)):
                part = mask[:, (k % 2) * 2 * P:(k % 2) * 2 * P + P]
                pool.affine_select(out=part, in_=part, compare_op=ALU.is_ge, fill=NEG, base=0,
                                   pattern=[[-1, P]], channel_multiplier=1).then_inc(consts_ready, 1)
            part = mask_window[:, P:2 * P]
            pool.affine_select(out=part, in_=part, compare_op=ALU.is_gt, fill=NEG, base=0,
                               pattern=[[1, P]], channel_multiplier=-1).then_inc(consts_ready, 1)

            for layer in range(2):
                pool.wait_ge(o_lo, KT * (layer + 1))
                pool.dma_start(gbc[:, :], rows[3 * layer].partition_broadcast(P)).then_inc(row_bc_loaded, 16)
                pool.wait_ge(h_ready, 16 * layer + 8)
                link(pool.memset(m[:, 0, :], 0.0))
                pool.memset(m[:, 1, :], 0.0).then_inc(m_zeroed, 1)
                pool.dma_start(gbc[:, :], rows[3 * layer + 1].partition_broadcast(P)).then_inc(row_bc_loaded, 16)
                pool.dma_start(p_raw, p_t[layer]).then_inc(p_loaded, 16)
                pool.wait_ge(h_ready, 16 * layer + 16)
                pool.dma_start(gbc[:, :], rows[3 * layer + 2].partition_broadcast(P)).then_inc(row_bc_loaded, 16)
            for c in range(CHUNKS - 1):
                for t in range(HALVES):
                    pool.wait_ge(row_done, ROWS_BEFORE_GATE[1] + HALVES * c + t + 1)
                    pool.dma_start(out[t * P:(t + 1) * P, c * CW:(c + 1) * CW], row[:, t, :]).then_inc(out_stored[t], 16)
            for t in range(HALVES):
                pool.wait_ge(out_stored[t], 16 * (CHUNKS - 1))

        @block.tensor
        def _(pe):
            lo_seen, used, half0 = Count(), Count(), Count()
            jobs = [Count(), Count()]
            rows_seen, h_seen = Count(), Count()
            split_n, plain_n = Count(), Count()
            slot = [0]

            def job(t, hi, lo, pairs, width=CW, need=None, after=None):
                if jobs[t].base:
                    pe.wait_ge(bank_free[t], jobs[t].at())
                jobs[t].add()
                tok = slice(t * P, (t + 1) * P)
                acc = ps[:, G[t], 0:width]
                for j in range(pairs):
                    s = (slot[0] + j) % RING
                    if t == 0:
                        pe.wait_ge(w_lo_ready, lo_seen.add())
                    if need and j in need:
                        pe.wait_ge(*need[j])
                    for k in range(2):
                        cols = slice(k * CW, k * CW + width)
                        kt = 2 * j + k
                        for n, (a, w) in enumerate(((hi, wh), (hi, wl), (lo, wh))):
                            last = pe.matmul(acc, a[:, kt, tok], w[:, s, cols],
                                             start=(kt == 0 and n == 0), stop=(kt == 2 * pairs - 1 and n == 2))
                    if t == 1:
                        last.then_inc(w_used, 1)
                        used.add()
                    elif j == pairs - 1:
                        last.then_inc(half0_done, 1)
                        half0.add()
                    if after and j in after:
                        after[j]()
                if t == 1:
                    slot[0] = (slot[0] + pairs) % RING

            def split_transpose(src, blocks=4):
                if split_n.base >= 2:
                    pe.wait_ge(split_lo_done, split_n.at(-1))
                b = T[split_n.base % 2]
                for i in range(blocks):
                    last = pe.transpose(ps[:, b, i * P:(i + 1) * P], src[:, i * P:(i + 1) * P], ident[:, :])
                last.then_inc(split_t_done, 1)
                split_n.add()

            def plain_transpose(src, blocks=4):
                if plain_n.base >= 2:
                    pe.wait_ge(plain_copied, plain_n.at(-1))
                b = L[plain_n.base % 2]
                for i in range(blocks):
                    last = pe.transpose(ps[:, b, i * P:(i + 1) * P], src[:, i * P:(i + 1) * P], ident[:, :])
                last.then_inc(plain_t_done, 1)
                plain_n.add()

            def row_split(t, blocks=4):
                pe.wait_ge(row_done, rows_seen.add())
                split_transpose(row[:, t, :], blocks)

            def row_plain(t, blocks=4, src=None):
                pe.wait_ge(row_done, rows_seen.add())
                plain_transpose(row[:, t, :] if src is None else src, blocks)

            def evacuated(t):
                pe.wait_ge(bank_free[t], jobs[t].at())

            def up_turn(c, t):
                if c < 4:
                    row_plain(t, 3)
                else:
                    pe.wait_ge(bank_free[t], 5 + c + 1)
                    plain_transpose(row[:, t, :], 2)

            def h_piece(t, i):
                pe.wait_ge(h_ready, h_seen.add())
                split_transpose(h[:, t, i * CW:(i + 1) * CW])

            def pieces(t, first):
                return {first + i: (lambda i=i: h_piece(t, i)) for i in range(4)}

            def pieces_ready(first):
                return {2 * i: (split_lo_done, first + i + 1) for i in range(4)}

            loop_counts = lambda extra, n=1: {lo_seen: 8 * n, used: 8 * n, half0: n, jobs[0]: n, jobs[1]: n, **extra}

            pe.wait_ge(consts_ready, 2)
            for j, t in [(j, t) for j in range(6) for t in range(HALVES)] + [(6, 0), (7, 0), (6, 1), (7, 1)]:
                if t == 0:
                    pe.wait_ge(w_lo_ready, lo_seen.add())
                    pe.wait_ge(x_lo, 2 * j + 2)
                if (j, t) == (7, 0):
                    pe.wait_ge(x_partial, 4)
                    for half in range(HALVES):
                        for n in range(4):
                            last = pe.matmul(ps[:, X_SUM[half], 0:1], x_part[:, n, half * P:(half + 1) * P],
                                             ones[:, :], start=n == 0, stop=n == 3)
                        last.then_inc(x_summed, 1)
                for kt in (2 * j, 2 * j + 1):
                    cols = slice((kt % 2) * CW, (kt % 2) * CW + CW)
                    for n, (a, w) in enumerate(((xh, wh), (xh, wl), (xl, wh))):
                        last = pe.matmul(ps[:, G[t], :], a[:, kt, t * P:(t + 1) * P], w[:, j, cols],
                                         start=(kt == 0 and n == 0), stop=(kt == KT - 1 and n == 2))
                if t == 1:
                    last.then_inc(w_used, 1)
                    used.add()
                elif j == 7:
                    last.then_inc(half0_done, 1)
                    half0.add()
            for t in range(HALVES):
                jobs[t].add()

            for c in range(1, 5):
                def turn_first():
                    pe.wait_ge(bank_free[0], 1)
                    split_transpose(row[:, 0, :])

                def turn_previous(c=c):
                    if c - 1 < 2:
                        pe.wait_ge(bank_free[1], c)
                        split_transpose(row[:, 1, :])
                    else:
                        row_plain(1)

                def turn_this(c=c):
                    if c < 2:
                        evacuated(0)
                        split_transpose(row[:, 0, :])
                    elif c < 4:
                        row_plain(0)
                    else:
                        row_plain(0, 3, doubled[0])
                before = {2: turn_first} if c == 1 else {}
                job(0, xh, xl, 8, IN_WIDTHS[c], after={**before, 5: turn_previous})
                job(1, xh, xl, 8, IN_WIDTHS[c], after={5: turn_this})

            def scores(n, q_parts, k_parts):
                if n >= len(S):
                    pe.wait_ge(s_masked, n + 1 - len(S))
                for a, b, keys in ((0, P, P), (P, 3 * P, 2 * P)):
                    tok = slice(0, P) if a == 0 else slice(P, 2 * P)
                    for i, (q, k) in enumerate(zip(q_parts, k_parts)):
                        last = pe.matmul(ps[:, S[n % len(S)], a:b], q[:, tok], k[:, 0:keys],
                                         start=(i == 0), stop=(i == len(q_parts) - 1))
                last.then_inc(s_done, 1)

            def turn_probs(n):
                pe.wait_ge(p_ready, n + 1)
                if n >= 2:
                    pe.wait_ge(pt_copied, n - 1)
                for i in range(3):
                    last = pe.transpose(ps[:, T[n % 2], i * P:(i + 1) * P], prob[n % PROBS][:, i * P:(i + 1) * P],
                                        ident[:, :])
                last.then_inc(pt_done, 1)

            def values(n, v, part, unit):
                pe.wait_ge(pt_copied, n + 1)
                if unit >= 2:
                    pe.wait_ge(o_lo, unit - 1)
                pe.matmul(ps[part, O[unit % 2], 0:SEQ], v(0), prob_t[n % 2][:, 0:SEQ], start=True, stop=False)
                last = pe.matmul(ps[part, O[unit % 2], P:SEQ], v(1), prob_t[n % 2][:, SEQ:SEQ + P], start=False, stop=True)
                last.then_inc(o_done, 1)

            def attention(first, heads, steps):
                for i in steps:
                    if i + 1 < len(heads):
                        scores(first + i + 1, heads[i + 1][0], heads[i + 1][1])
                    if 2 <= i < len(heads) + 2:
                        turn_probs(first + i - 2)
                    if i >= 3:
                        values(first + i - 3, *heads[i - 3][2:])

            heads = []
            for hd in range(SWA_H):
                part = slice(64 * (hd % 2), 64 * (hd % 2) + 64)
                kv = hd // (SWA_H // SWA_KV)
                heads.append(((swa_q[part, hd // 2, :],), (swa_k[part, kv, :],),
                              lambda blk, kv=kv: swa_v[:, blk, kv * 64:kv * 64 + 64], part, hd // 2))
            for hd in range(MLA_H):
                part = slice(64 * (hd % 2), 64 * (hd % 2) + 64)
                heads.append(((mla_q[:, hd // 2, hd % 2, :], mla_q[part, hd // 2, 2, :]),
                              (mla_k[:, hd, :], swa_k[part, 2, :]),
                              lambda blk, hd=hd: vm[:, blk, hd * 128:hd * 128 + 128],
                              slice(0, P), SWA_H // 2 + hd))

            q_latent = (al[:, 0:4, :], al[:, 4:8, :])
            kv_latent = (al[:, 8:12, :], al[:, 12:16, :])
            swa_turned = plain_n.at(1)
            for c in range(8):
                lhs, width = (q_latent, Q_UP_W) if c < 4 else (kv_latent, CW)
                need = {0: (split_lo_done, 2 if c < 4 else 4)} if c % 4 == 0 else None
                if c == 7:
                    pe.wait_ge(plain_copied, swa_turned)
                    attention(0, heads, range(-1, 0))
                job(0, *lhs, 2, width, need=need, after={0: lambda: up_turn(c - 1, 0)} if c else None)
                if c == 7:
                    attention(0, heads, range(0, 1))
                job(1, *lhs, 2, width,
                    after={0: (lambda: up_turn(c - 1, 1)) if c else (lambda: row_plain(1, 3, doubled[1]))})
            up_turn(7, 0)
            up_turn(7, 1)
            pe.wait_ge(plain_copied, plain_n.at())
            attention(0, heads, range(1, 2))
            pe.wait_ge(split_lo_done, split_n.at())
            pe.wait_ge(bank_free[0], jobs[0].at())
            pe.wait_ge(bank_free[1], jobs[1].at())
            attention(0, heads, range(2, len(heads) + 3))

            def mixer_out_and_mlp(layer):
                first = layer * KT
                job(0, xh, xl, 8, need={j: (o_lo, first + 2 * j + 2) for j in range(8)})
                job(1, xh, xl, 8)
                with repeat(pe, 2, loop_counts({})):
                    job(0, xh, xl, 8)
                    job(1, xh, xl, 8)
                job(0, xh, xl, 8)
                s0 = split_n.at()
                job(1, xh, xl, 8, after=pieces(0, 2))
                job(0, xh, xl, 8, need=pieces_ready(s0), after=pieces(1, 3))
                job(1, xh, xl, 8, need=pieces_ready(s0 + 4), after={2: lambda: row_split(0)})

                def up_rest():
                    with repeat(pe, 3, loop_counts({split_n: 2, rows_seen: 2})):
                        job(0, xh, xl, 8, after={2: lambda: row_split(1)})
                        job(1, xh, xl, 8, after={2: lambda: row_split(0)})

                def down(times, first):
                    if first:
                        n = split_n.at()
                        job(0, ah, al, 8, need={6: (split_lo_done, n)}, after={2: lambda: row_split(1)})
                        job(1, ah, al, 8, need={6: (split_lo_done, split_n.at())})
                    with repeat(pe, times, loop_counts({})):
                        job(0, ah, al, 8)
                        job(1, ah, al, 8)

                with repeat(pe, 3, loop_counts({split_n: 8, rows_seen: 8}, 8)):
                    up_rest()
                    down(3, True)
                    job(0, xh, xl, 8)
                    job(1, xh, xl, 8, after={2: lambda: row_split(0)})
                up_rest()
                down(2, True)
                job(0, ah, al, 8)
                s1 = split_n.at()
                job(1, ah, al, 8, after=pieces(0, 3))
                pe.wait_ge(p_lo, layer + 1)
                for c in range(CHUNKS):
                    job(0, xh, xl, 1)
                    job(1, xh, xl, 1)
                turn = layer == 0
                job(0, ah, al, 8, need=pieces_ready(s1), after=pieces(1, 0))
                job(1, ah, al, 8, need=pieces_ready(s1 + 4), after={5: lambda: row_split(0)} if turn else None)
                with repeat(pe, 3, loop_counts({split_n: 2, rows_seen: 2} if turn else {})):
                    job(0, ah, al, 8, after={5: lambda: row_split(1)} if turn else None)
                    job(1, ah, al, 8, after={5: lambda: row_split(0)} if turn else None)

            mixer_out_and_mlp(0)

            n = split_n.at()
            job(0, xh, xl, 8, need={6: (split_lo_done, n)}, after={2: lambda: row_split(1)})
            job(1, xh, xl, 8, need={6: (split_lo_done, split_n.at())}, after={5: lambda: row_plain(0)})
            with repeat(pe, 7, loop_counts({plain_n: 2, rows_seen: 2})):
                job(0, xh, xl, 8, after={5: lambda: row_plain(1)})
                job(1, xh, xl, 8, after={5: lambda: row_plain(0)})
            job(0, xh, xl, 8, after={5: lambda: row_plain(1)})
            job(1, xh, xl, 8)
            with repeat(pe, 2, loop_counts({})):
                job(0, xh, xl, 8)
                job(1, xh, xl, 8)
            n0 = SWA_H + MLA_H
            heads = [((moba_qk[:, hd, :],), (moba_qk[:, MOBA_H + hd, :],),
                      lambda blk, hd=hd: m[:, blk, hd * 128:hd * 128 + 128],
                      slice(0, P), KT + hd) for hd in range(MOBA_H)]
            job(0, xh, xl, 8)
            pe.wait_ge(plain_copied, plain_n.at())
            job(1, xh, xl, 8, after={2 + i: (lambda i=i: attention(n0, heads, range(i - 1, i))) for i in range(3)})
            attention(n0, heads, range(2, 3))
            pe.wait_ge(bank_free[0], jobs[0].at())
            pe.wait_ge(bank_free[1], jobs[1].at())
            attention(n0, heads, range(3, len(heads) + 3))
            mixer_out_and_mlp(1)

        @block.scalar
        def _(act):
            conv, half0, used, sq, split_n, plain_n = (Count() for _ in range(6))
            raw_seen = [Count() for _ in range(RAW)]
            jobs = [Count(), Count()]
            var_seen, rstd_seen, h_seen, rows_seen = (Count() for _ in range(4))

            def hi(width=CW):
                n = conv.base
                act.wait_ge(raw_loaded[n % RAW], raw_seen[n % RAW].add(16))
                if n >= RING:
                    act.wait_ge(w_used, conv.at(1 - RING))
                src = raw[:, n % RAW, :].rearrange("p (k c) -> p k c", k=2)[:, :, 0:width]
                dst = wh[:, n % RING, :].rearrange("p (k c) -> p k c", k=2)[:, :, 0:width]
                act.activation(dst, src, ACT.Copy).then_inc(w_hi_ready, 1)
                conv.add()

            def hi_steps(n=1):
                return {conv: 8 * n, half0: n, used: 8 * n, jobs[0]: n, jobs[1]: n,
                        **{raw_seen[i]: 32 * n for i in range(RAW)}}

            def job_done(t, pairs=8):
                if t == 0:
                    act.wait_ge(half0_done, half0.add())
                else:
                    act.wait_ge(w_used, used.add(pairs))
                jobs[t].add()

            def square(src, accum):
                if sq.base:
                    act.wait_ge(sq_done, sq.at())
                act.activation(ps[:, JUNK, 0:CW], src, ACT.Square, accum_out=accum).then_inc(sq_done, 1)
                sq.add()

            def root():
                act.wait_ge(var_ready, var_seen.add())
                act.activation(std, var, ACT.Sqrt).then_inc(std_ready, 1)

            def scaled_row(t, norm, width=CW):
                act.activation(row[:, t, 0:width], ps[:, G[t], 0:width], ACT.Copy,
                               scale=rstd(norm, t)).then_inc(bank_free[t], 1)

            def split_hi(dst, t, gain=None):
                act.wait_ge(split_t_done, split_n.add())
                b = T[(split_n.base - 1) % 2]
                tok = slice(t * P, (t + 1) * P)
                if gain is None:
                    act.activation(dst[:, :, tok], ps[:, b, :].rearrange("p (k s) -> p k s", k=4), ACT.Copy)\
                       .then_inc(split_hi_done, 1)
                    return
                for i in range(4):
                    last = act.activation(dst[:, i, tok], ps[:, b, i * P:(i + 1) * P], ACT.Copy,
                                          scale=gt[:, gain + i:gain + i + 1])
                last.then_inc(split_hi_done, 1)

            def plain_copy(dst, t, blocks):
                act.wait_ge(plain_t_done, plain_n.add())
                b = L[(plain_n.base - 1) % 2]
                act.activation(dst[:, :, t * P:(t + 1) * P],
                               ps[:, b, 0:blocks * P].rearrange("p (k s) -> p k s", k=blocks), ACT.Copy)\
                   .then_inc(plain_copied, 1)

            act.wait_ge(consts_ready, 1)
            act.activation(warm[:, :], ones[:, :], ACT.Copy)
            hi()
            act.wait_ge(gains_loaded, 16)
            for n in range(4):
                for kt in range(4 * n, 4 * n + 4):
                    if kt in xt_loaded:
                        act.wait_ge(xt_loaded[kt], 16)
                    act.activation(xh[:, kt, :], x_raw[:, kt, :], ACT.Copy, scale=gt[:, kt:kt + 1]).then_inc(x_hi, 1)
                if n:
                    hi()
                act.activation(x_sq[:, 4 * n:4 * n + 4, :], x_raw[:, 4 * n:4 * n + 4, :], ACT.Square)\
                   .then_inc(x_squared, 1)
                hi()
            for _ in range(EARLY):
                hi()
            for t in range(HALVES):
                root()
            act.wait_ge(rstd_ready, rstd_seen.add(2))

            for c in range(5):
                for t in range(HALVES):
                    nexts = (IN_WIDTHS + (Q_UP_W,))[c + 1]
                    job_done(t)
                    if c < 4:
                        scaled_row(t, N_PRE0)
                    else:
                        act.activation(row[:, t, 0:192], ps[:, G[t], 0:192], ACT.Copy, scale=rstd(N_PRE0, t))
                        act.activation(swa_v[:, t, :], ps[:, G[t], 192:320], ACT.Copy,
                                       scale=rstd(N_PRE0, t)).then_inc(bank_free[t], 1)
                    if c < 2:
                        act.wait_ge(bank_free[t], jobs[t].at())
                        square(row[:, t, :], ssq(N_Q + c, t, 0, 1))
                        root()
                    for _ in range((5, 3)[t] if c else (1, 7 - EARLY)[t]):
                        hi(nexts)
                    if c < 2:
                        split_hi(al[:, 8 * c:8 * c + 4, :], t, gain=64 + 4 * c)
                    elif c < 4:
                        plain_copy(swa_q[:, 4 * c - 8:4 * c - 4, :], t, 4)
                    elif t == 0:
                        plain_copy(swa_k, t, 3)
                if c == 1:
                    act.wait_ge(angles_ready, 1)
                    act.activation(angles, angles, ACT.Sin).then_inc(sines_ready, 1)

            def exps(n, sink=None):
                act.wait_ge(nmax_ready, n + 1)
                for t, (a, b) in enumerate(((0, P), (P, 3 * P))):
                    last = act.activation(prob[n % PROBS][:, a:b], prob[n % PROBS][:, a:b], ACT.Exp,
                                          bias=nmax[n % 3][:, t:t + 1], accum_out=rsum[n % 3][:, t:t + 1])
                if sink is not None:
                    last = act.activation(esink[n % 3], nmax[n % 3], ACT.Exp, bias=sinkv[:, sink:sink + 1])
                last.then_inc(exp_done, 1)

            def copy_probs(n):
                act.wait_ge(pt_done, n + 1)
                if n >= 2:
                    act.wait_ge(o_done, n - 1)
                act.activation(prob_t[n % 2], ps[:, T[n % 2], 0:3 * P], ACT.Copy).then_inc(pt_copied, 1)

            def out_hi(n, kt):
                act.wait_ge(o_done, n + 1)
                act.activation(xh[:, kt, :], ps[:, O[kt % 2], 0:SEQ], ACT.Copy).then_inc(o_hi, 1)

            def attention(first, heads, steps):
                for i in steps:
                    if i >= 4 and heads[i - 4][1] is not None:
                        out_hi(first + i - 4, heads[i - 4][1])
                    if i < len(heads):
                        exps(first + i, heads[i][0])
                    if 2 <= i < len(heads) + 2:
                        copy_probs(first + i - 2)

            heads = [(hd, hd // 2 if hd % 2 else None) for hd in range(SWA_H)] \
                + [(None, SWA_H // 2 + hd) for hd in range(MLA_H)]

            act.wait_ge(rstd_ready, rstd_seen.add(4))

            def turned(c, t):
                if c < 4:
                    plain_copy(mla_q[:, c, :, :], t, 3)
                else:
                    plain_copy(mla_k[:, 2 * c - 8:2 * c - 6, :], t, 2)

            for c in range(8):
                for t in range(HALVES):
                    if c:
                        turned(c - 1, t)
                    elif t == 1:
                        plain_copy(swa_k, t, 3)
                    job_done(t, 2)
                    if c < 4:
                        scaled_row(t, N_Q, Q_UP_W)
                    else:
                        act.activation(row[:, t, 0:256], ps[:, G[t], 0:256], ACT.Copy, scale=rstd(N_KV, t))
                        act.activation(vm[:, t, (c - 4) * 256:(c - 3) * 256], ps[:, G[t], 256:512], ACT.Copy,
                                       scale=rstd(N_KV, t)).then_inc(bank_free[t], 1)
                    if t == 1 and c < 7:
                        hi()
                        hi()
                    if t == 0 and c == 7:
                        attention(0, heads, range(1))
            turned(7, 0)
            turned(7, 1)
            attention(0, heads, range(1, len(heads) + 4))
            hi()
            hi()


            def split_h(t, pre, gain, dst, pairs):
                for i in range(4):
                    h_seen.add()
                    if pre is not None:
                        act.wait_ge(h_ready, h_seen.at())
                        square(h[:, t, i * CW:(i + 1) * CW], ssq(pre, t, i, i + 1))
                    split_hi(dst[:, 4 * i:4 * i + 4, :], t, None if gain is None else gain + 4 * i)
                    for _ in range(pairs[i]):
                        hi()
                if pre is not None:
                    root()

            def block_rest(layer):
                post, mpre, mpost = ((N_POST0, N_MPRE0, N_MPOST0), (N_POST1, N_MPRE1, N_MPOST1))[layer]
                last_layer = layer == 1

                def out_chunk(i, last):
                    for t in range(HALVES):
                        job_done(t)
                        square(ps[:, G[t], :], stats[:, bass.ds(i + (10 * post + 5 * t), 1)])
                        todo = 5 if t == 0 else 3
                        if last:
                            root()
                            hi()
                            split_h(t, mpre, 16 * (2 + layer), xh, OUT_PAIRS[t])
                        else:
                            for _ in range(todo):
                                hi()

                with repeat(act, 3, {**hi_steps(), sq: 2}) as i:
                    out_chunk(i, False)
                out_chunk(3, True)

                act.wait_ge(rstd_ready, rstd_seen.add(4))

                def up(i):
                    for t in range(HALVES):
                        job_done(t)
                        act.activation(row[:, t, :], ps[:, G[t], :], ACT.Relu, scale=rstd(mpre, t))\
                           .then_inc(bank_free[t], 1)
                        hi()
                        hi()
                        split_hi(ah[:, bass.ds(i * 4, 4), :], t)
                        for _ in range(3 if t == 0 else 1):
                            hi()

                def ups():
                    with repeat(act, 4, {**hi_steps(), split_n: 2}) as i:
                        up(i)

                with repeat(act, 3, {**hi_steps(8), split_n: 8}):
                    ups()
                    with repeat(act, 4, hi_steps()):
                        for t in range(HALVES):
                            job_done(t)
                            for _ in range(5 if t == 0 else 3):
                                hi()
                ups()
                act.wait_ge(p_loaded, 16 * layer + 16)
                act.activation(xh[:, 0:2, :], p_raw, ACT.Copy).then_inc(p_hi, 1)

                def last_down(i, last):
                    for t in range(HALVES):
                        job_done(t)
                        act.wait_ge(bank_free[t], jobs[t].at())
                        square(m[:, t, bass.ds(i * CW, CW)], stats[:, bass.ds(i + (10 * mpost + 5 * t), 1)])
                        if not last:
                            for _ in range(5 if t == 0 else 3):
                                hi()
                        else:
                            root()
                            hi()
                            if t == 0:
                                split_h(t, None, None, ah, DOWN_PAIRS)

                with repeat(act, 3, {**hi_steps(), sq: 2}) as i:
                    last_down(i, False)
                last_down(3, True)

                for c in range(CHUNKS):
                    for t in range(HALVES):
                        job_done(t, 1)
                        dst = m[:, 0, :] if t == 0 else proj1
                        act.activation(dst[:, c * CW:(c + 1) * CW], ps[:, G[t], :], ACT.Copy).then_inc(bank_free[t], 1)
                    hi()
                split_h(1, None, None, ah, (1, 1, 0, 0))

                def gate(i, convert=True):
                    for t in range(HALVES):
                        job_done(t)
                        act.wait_ge(bank_free[t], jobs[t].at())
                        act.activation(row[:, t, :], row[:, t, :], ACT.Sigmoid).then_inc(sig_done, 1)
                        todo = (5 if t == 0 else 3) if convert else 0
                        for _ in range(min(todo, 1)):
                            hi()
                        rows_seen.add()
                        if not last_layer:
                            act.wait_ge(row_done, rows_seen.at())
                            act.activation(h[:, t, bass.ds(i * CW, CW)], row[:, t, :], ACT.Copy).then_inc(h_saved, 1)
                            square(row[:, t, :], stats[:, bass.ds(i + (10 * N_PRE1 + 5 * t), 1)])
                        for _ in range(todo - min(todo, 1)):
                            hi()
                        if not last_layer:
                            act.wait_ge(split_t_done, split_n.add())
                            b = T[(split_n.base - 1) % 2]
                            tok = slice(t * P, (t + 1) * P)
                            for k in range(4):
                                last = act.activation(xh[:, bass.ds(i * 4 + k, 1), tok],
                                                      ps[:, b, k * P:(k + 1) * P].unsqueeze(1),
                                                      ACT.Copy, scale=gt[:, bass.ds(i * 4 + (16 + k), 1)])
                            last.then_inc(split_hi_done, 1)

                if not last_layer:
                    with repeat(act, 4, {**hi_steps(), sq: 2, split_n: 2, rows_seen: 2}) as i:
                        gate(i)
                    root()
                    root()
                    act.wait_ge(rstd_ready, rstd_seen.add(4))
                else:
                    with repeat(act, 3, {**hi_steps(), rows_seen: 2}) as i:
                        gate(i)
                    gate(3, False)

            rows_seen.add(ROWS_BEFORE_GATE[0])
            block_rest(0)

            with repeat(act, 8, {**hi_steps(), plain_n: 2}) as i:
                for t in range(HALVES):
                    job_done(t)
                    scaled_row(t, N_PRE1)
                    for _ in range(5 if t == 0 else 3):
                        hi()
                    plain_copy(moba_qk[:, bass.ds(i * 4, 4), :], t, 4)

            def v_rows(i, t):
                job_done(t)
                act.activation(m[:, t, bass.ds(i * CW, CW)], ps[:, G[t], :], ACT.Copy,
                               scale=rstd(N_PRE1, t)).then_inc(bank_free[t], 1)

            with repeat(act, 3, hi_steps()) as i:
                for t in range(HALVES):
                    v_rows(i, t)
                    for _ in range(5 if t == 0 else 3):
                        hi()
            heads = [(None, hd) for hd in range(MOBA_H)]
            v_rows(3, 0)
            for pairs, step in ODD_START:
                for _ in range(pairs):
                    hi()
                attention(SWA_H + MLA_H, heads, range(step, step + 1))
            v_rows(3, 1)
            attention(SWA_H + MLA_H, heads, range(len(ODD_START), len(heads) + 4))
            for _ in range(8 - sum(pairs for pairs, _ in ODD_START)):
                hi()
            rows_seen.add(ROWS_BEFORE_GATE[1] - rows_seen.base)
            block_rest(1)
            assert conv.base == PAIRS

        @block.vector
        def _(dve):
            conv, half0, used, sq, split_n = (Count() for _ in range(5))
            jobs = [Count(), Count()]
            steps, roots, rows_out, h_out, sigs = (Count() for _ in range(5))

            def link(ins):
                ins.then_inc(dve_step, 1)
                dve.wait_ge(dve_step, steps.add())

            def lo(width=CW):
                n = conv.base
                dve.wait_ge(w_hi_ready, conv.add())
                k = lambda ap: ap.rearrange("p (k c) -> p k c", k=2)[:, :, 0:width]
                dve.tensor_tensor(k(wl[:, n % RING, :]), k(raw[:, n % RAW, :]), k(wh[:, n % RING, :].bitcast(F32)),
                                  ALU.subtract).then_inc(w_lo_ready, 1)

            def lo_steps(n=1):
                return {conv: 8 * n, half0: n, used: 8 * n, jobs[0]: n, jobs[1]: n}

            def job_done(t, pairs=8):
                if t == 0:
                    dve.wait_ge(half0_done, half0.add())
                else:
                    dve.wait_ge(w_used, used.add(pairs))
                jobs[t].add()

            def skip_job(t, pairs=8):
                if t == 0:
                    half0.add()
                else:
                    used.add(pairs)
                jobs[t].add()

            def variance(norm, t, n, dim):
                dve.wait_ge(sq_done, sq.at())
                src = ssq(norm, t, 0, 1)
                if n > 1:
                    link(dve.tensor_reduce(var, ssq(norm, t, 0, n), AX, ALU.add))
                    src = var
                dve.tensor_scalar(var, src, 1.0 / dim, EPS, ALU.mult, ALU.add).then_inc(var_ready, 1)
                roots.add()

            def inverse_root(norm, t):
                dve.wait_ge(std_ready, roots.at())
                link(dve.reciprocal(rec, std))
                link(dve.scalar_tensor_tensor(cor, rec, rec, var, ALU.mult, ALU.mult))
                link(dve.tensor_scalar(cor, cor, -0.5, 1.5, ALU.mult, ALU.add))
                dve.tensor_tensor(rstd(norm, t), cor, rec, ALU.mult).then_inc(rstd_ready, 1)
                dve.wait_ge(rstd_ready, roots.at())

            def split_lo(dst, dst_hi, t, gain=None):
                dve.wait_ge(split_hi_done, split_n.add())
                b = T[(split_n.base - 1) % 2]
                tok = slice(t * P, (t + 1) * P)
                if gain is None:
                    dve.tensor_tensor(dst[:, :, tok], ps[:, b, :].rearrange("p (k s) -> p k s", k=4),
                                      dst_hi[:, :, tok].bitcast(F32), ALU.subtract).then_inc(split_lo_done, 1)
                    return
                for i in range(4):
                    last = dve.scalar_tensor_tensor(dst[:, i, tok], ps[:, b, i * P:(i + 1) * P],
                                                    gt[:, gain + i:gain + i + 1], dst_hi[:, i, tok].bitcast(F32),
                                                    ALU.mult, ALU.subtract)
                last.then_inc(split_lo_done, 1)

            def rope(t, a, n, half, cos, sin, dst=None):
                r = row[:, t, a:a + 2 * n * half].rearrange("p (n j d) -> p n j d", n=n, j=2)
                s = tmp[:, 0:2 * n * half].rearrange("p (n j d) -> p n j d", n=n, j=2)
                for j in range(2):
                    part = sin[:, t, j, :].unsqueeze(1).to_broadcast([P, n, half])
                    link(dve.tensor_tensor(s[:, :, j, :], r[:, :, 1 - j, :], part, ALU.mult))
                both = cos[:, t, :].unsqueeze(1).unsqueeze(1).to_broadcast([P, n, 2, half])
                link(dve.tensor_tensor(r, r, both, ALU.mult))
                if dst is None:
                    dve.tensor_tensor(r, r, s, ALU.add).then_inc(row_done, 1)
                else:
                    d = dst.rearrange("p (n two c) -> p n two c", n=n, two=2)
                    flat = lambda ap: ap.rearrange("p n j d -> p n (j d)")
                    link(dve.tensor_tensor(d[:, :, 0, :], flat(r), flat(s), ALU.add))
                    dve.tensor_tensor(d[:, :, 1, :], flat(r), flat(s), ALU.add).then_inc(row_done, 1)
                rows_out.add()
                dve.wait_ge(row_done, rows_out.at())

            lo()
            dve.wait_ge(gains_loaded, 16)
            for n in range(4):
                for kt in range(4 * n, 4 * n + 4):
                    dve.wait_ge(x_hi, kt + 1)
                    dve.scalar_tensor_tensor(xl[:, kt, :], x_raw[:, kt, :], gt[:, kt:kt + 1],
                                             xh[:, kt, :].bitcast(F32), ALU.mult, ALU.subtract).then_inc(x_lo, 1)
                if n:
                    lo()
                lo()
                dve.wait_ge(x_squared, n + 1)
                dve.tensor_reduce(x_part[:, n, :], x_sq[:, 4 * n:4 * n + 4, :].rearrange("p k s -> p s k"),
                                  AX, ALU.add).then_inc(x_partial, 1)
            for _ in range(EARLY):
                lo()
            for t in range(HALVES):
                dve.wait_ge(x_summed, t + 1)
                dve.tensor_scalar(var, ps[:, X_SUM[t], 0:1], 1.0 / D, EPS, ALU.mult, ALU.add).then_inc(var_ready, 1)
                roots.add()
                inverse_root(N_PRE0, t)

            ang, fold = angles[:, 0:192], angles[:, 192:384]

            def rope_angles():
                dve.wait_ge(tables_loaded, 48)
                posf = stats[:, 120:122]
                turns_i, turns = gbc[:, 384:576].bitcast(I32), gbc[:, 576:768]
                link(dve.tensor_copy(posf, pos_i[:, :]))
                for t in range(HALVES):
                    link(dve.tensor_scalar(ang[:, 96 * t:96 * t + 96], tmp[:, 0:96], posf[:, t:t + 1], None, ALU.mult))
                link(dve.tensor_scalar(turns_i, ang, 1.0 / TWO_PI, None, ALU.mult))
                link(dve.tensor_copy(turns, turns_i))
                for part in (PI_A, PI_B, PI_C):
                    link(dve.scalar_tensor_tensor(ang, turns, -part, ang, ALU.mult, ALU.add))
                link(dve.tensor_scalar(ang, ang, PI_MAX, -PI_MAX, ALU.min, ALU.max))
                link(dve.scalar_tensor_tensor(fold, ang, -1.0, ang, ALU.mult, ALU.max))
                dve.tensor_scalar(fold, fold, -1.0, float(np.pi / 2), ALU.mult, ALU.add).then_inc(angles_ready, 1)
                link(dve.tensor_scalar(nsink[:, 0:SWA_H], sinkv, -1.0, None, ALU.mult))

            def rope_tables():
                dve.wait_ge(sines_ready, 1)
                s3 = ang.rearrange("p (t f) -> p t f", t=2)
                c3 = fold.rearrange("p (t f) -> p t f", t=2)
                dve.tensor_copy(cos128[:, :, :], c3[:, :, 0:64])
                dve.tensor_copy(cos64[:, :, :], c3[:, :, 64:96])
                dve.tensor_copy(sin128[:, :, 1, :], s3[:, :, 0:64])
                dve.tensor_copy(sin64[:, :, 1, :], s3[:, :, 64:96])
                dve.tensor_scalar(sin128[:, :, 0, :], s3[:, :, 0:64], -1.0, None, ALU.mult)
                dve.tensor_scalar(sin64[:, :, 0, :], s3[:, :, 64:96], -1.0, None, ALU.mult).then_inc(angles_ready, 1)
                dve.wait_ge(angles_ready, 2)

            for c in range(5):
                for t in range(HALVES):
                    nexts = (IN_WIDTHS + (Q_UP_W,))[c + 1]
                    skip_job(t)
                    if c < 2:
                        sq.add()
                        variance(N_Q + c, t, 1, RANK)
                        inverse_root(N_Q + c, t)
                    else:
                        dve.wait_ge(bank_free[t], jobs[t].at())
                        if c < 4:
                            rope(t, 0, 8, 32, cos64, sin64)
                        else:
                            rope(t, 0, 3, 32, cos64, sin64, doubled[t])
                    for _ in range((5, 3)[t] if c else (1, 7 - EARLY)[t]):
                        lo(nexts)
                    if c < 2:
                        split_lo(al[:, 8 * c + 4:8 * c + 8, :], al[:, 8 * c:8 * c + 4, :], t, gain=64 + 4 * c)
                if c == 0:
                    rope_angles()
                if c == 1:
                    rope_tables()

            def mark(ins):
                ins.then_inc(dve_step, 1)
                return steps.add()

            def softmax_step(new, old):
                n, scale, mask, sink = new or (None,) * 4
                o, o_sink = old or (None, None)
                if new:
                    p, top = prob[n % PROBS], nmax[n % 3]
                    dve.wait_ge(s_done, n + 1)
                    if n >= PROBS:
                        dve.wait_ge(pt_done, n + 1 - PROBS)
                    dve.scalar_tensor_tensor(p, ps[:, S[n % len(S)], 0:3 * P], scale, mask[:, :], ALU.mult, ALU.add)\
                       .then_inc(s_masked, 1)
                if old:
                    q, total, inv = prob[o % PROBS], rsum[o % 3], rinv[o % 3]
                    dve.wait_ge(exp_done, o + 1)
                    if o_sink is not None:
                        summed = mark(dve.tensor_tensor(total, total, esink[o % 3], ALU.add))
                if new:
                    dve.wait_ge(s_masked, n + 1)
                    dve.tensor_reduce(top[:, 0:1], p[:, 0:P], AX, ALU.max, negate=True)
                if old:
                    if o_sink is not None:
                        dve.wait_ge(dve_step, summed)
                    inverted = mark(dve.reciprocal(inv, total))
                if new:
                    last = dve.tensor_reduce(top[:, 1:2], p[:, P:3 * P], AX, ALU.max, negate=True)
                    if sink is None:
                        last.then_inc(nmax_ready, 1)
                    else:
                        topped = mark(last)
                if old:
                    dve.wait_ge(dve_step, inverted)
                    dve.tensor_scalar(q[:, 0:P], q[:, 0:P], inv[:, 0:1], None, ALU.mult)
                if new and sink is not None:
                    dve.wait_ge(dve_step, topped)
                    dve.tensor_scalar(top, top, nsink[:, sink:sink + 1], None, ALU.min).then_inc(nmax_ready, 1)
                if old:
                    dve.tensor_scalar(q[:, P:3 * P], q[:, P:3 * P], inv[:, 1:2], None, ALU.mult).then_inc(p_ready, 1)

            splits = Count()

            def out_lo(kt):
                dve.wait_ge(o_hi, splits.add())
                dve.tensor_tensor(xl[:, kt, :], ps[:, O[kt % 2], 0:SEQ], xh[:, kt, :].bitcast(F32),
                                  ALU.subtract).then_inc(o_lo, 1)

            def attention(first, heads, steps):
                for i in steps:
                    softmax_step((first + i, *heads[i][0:3]) if i < len(heads) else None,
                                 (first + i - 1, heads[i - 1][2]) if 1 <= i <= len(heads) else None)
                    if i >= 4 and heads[i - 4][3] is not None:
                        out_lo(heads[i - 4][3])

            heads = [(SWA_D ** -0.5, mask_window, hd, hd // 2 if hd % 2 else None) for hd in range(SWA_H)] \
                + [((NOPE + ROPE) ** -0.5, mask_causal, None, SWA_H // 2 + hd) for hd in range(MLA_H)]

            dve.wait_ge(consts_ready, 7)
            for c in range(8):
                for t in range(HALVES):
                    skip_job(t, 2)
                    if c < 4:
                        dve.wait_ge(bank_free[t], jobs[t].at())
                        rope(t, 2 * NOPE, 2, 32, cos64, sin64)
                    if t == 1 and c < 7:
                        lo()
                        lo()
            attention(0, heads, range(len(heads) + 4))
            lo()
            lo()

            def update_h(t, post, scale_piece):
                variance(post, t, 4, D)
                scale_piece()
                inverse_root(post, t)
                for i in range(4):
                    cols = slice(i * CW, (i + 1) * CW)
                    dve.scalar_tensor_tensor(h[:, t, cols], m[:, t, cols], rstd(post, t), h[:, t, cols],
                                             ALU.mult, ALU.add).then_inc(h_ready, 1)
                h_out.add(4)
                lo()

            def split_h(t, pre, gain, dst_hi, dst_lo, pairs):
                for i in range(4):
                    split_lo(dst_lo[:, 4 * i:4 * i + 4, :], dst_hi[:, 4 * i:4 * i + 4, :], t,
                             None if gain is None else gain + 4 * i)
                    for _ in range(pairs[i]):
                        lo()
                if pre is not None:
                    sq.add(4)
                    variance(pre, t, 4, D)
                    inverse_root(pre, t)

            def block_rest(layer):
                post, mpre, mpost = ((N_POST0, N_MPRE0, N_MPOST0), (N_POST1, N_MPRE1, N_MPOST1))[layer]
                last_layer = layer == 1

                dve.wait_ge(row_bc_loaded, 16 * (3 * layer + 1))
                if layer == 0:
                    dve.wait_ge(x_loaded, 16)
                else:
                    dve.wait_ge(h_saved, HALVES * CHUNKS)

                def out_chunk(i, last):
                    for t in range(HALVES):
                        def scale_piece():
                            cols = bass.ds(i * CW, CW)
                            dve.tensor_tensor(m[:, t, cols], ps[:, G[t], :], gbc[:, cols], ALU.mult)\
                               .then_inc(bank_free[t], 1)

                        skip_job(t)
                        sq.add()
                        dve.wait_ge(sq_done, sq.at())
                        if last:
                            update_h(t, post, lambda: (scale_piece(), dve.wait_ge(bank_free[t], jobs[t].at())))
                            split_h(t, mpre, 16 * (2 + layer), xh, xl, OUT_PAIRS[t])
                        else:
                            scale_piece()
                            for _ in range(5 if t == 0 else 3):
                                lo()

                with repeat(dve, 3, {**lo_steps(), sq: 2}) as i:
                    out_chunk(i, False)
                out_chunk(3, True)

                def ups():
                    with repeat(dve, 4, {**lo_steps(), split_n: 2, rows_out: 2}) as i:
                        for t in range(HALVES):
                            skip_job(t)
                            dve.wait_ge(bank_free[t], jobs[t].at())
                            dve.tensor_tensor(row[:, t, :], row[:, t, :], row[:, t, :], ALU.mult).then_inc(row_done, 1)
                            rows_out.add()
                            lo()
                            lo()
                            split_lo(al[:, bass.ds(i * 4, 4), :], ah[:, bass.ds(i * 4, 4), :], t)
                            for _ in range(3 if t == 0 else 1):
                                lo()

                def add_down(i, t):
                    dve.wait_ge(bank_free[t], jobs[t].at())
                    job_done(t)
                    cols = bass.ds(i * CW, CW)
                    dve.tensor_tensor(m[:, t, cols], ps[:, G[t], :], m[:, t, cols], ALU.add).then_inc(bank_free[t], 1)

                dve.wait_ge(m_zeroed, layer + 1)
                with repeat(dve, 3, {**lo_steps(8), split_n: 8, rows_out: 8}):
                    ups()
                    with repeat(dve, 4, lo_steps()) as i:
                        for t in range(HALVES):
                            add_down(i, t)
                            for _ in range(5 if t == 0 else 3):
                                lo()
                ups()
                dve.wait_ge(p_hi, layer + 1)
                dve.tensor_tensor(xl[:, 0:2, :], p_raw, xh[:, 0:2, :].bitcast(F32), ALU.subtract).then_inc(p_lo, 1)
                dve.wait_ge(row_bc_loaded, 16 * (3 * layer + 2))

                def last_down(i, last):
                    for t in range(HALVES):
                        def scale_piece():
                            cols = bass.ds(i * CW, CW)
                            link(dve.tensor_tensor(m[:, t, cols], m[:, t, cols], gbc[:, cols], ALU.mult))

                        add_down(i, t)
                        sq.add()
                        if not last:
                            lo()
                            dve.wait_ge(sq_done, sq.at())
                            scale_piece()
                            for _ in range(4 if t == 0 else 2):
                                lo()
                        else:
                            update_h(t, mpost, scale_piece)
                            if t == 0:
                                split_h(t, None, None, ah, al, DOWN_PAIRS)

                with repeat(dve, 3, {**lo_steps(), sq: 2, steps: 2}) as i:
                    last_down(i, False)
                last_down(3, True)

                for c in range(CHUNKS):
                    for t in range(HALVES):
                        skip_job(t, 1)
                    lo()
                split_h(1, None, None, ah, al, (1, 1, 0, 0))
                dve.wait_ge(h_ready, h_out.at())

                dve.wait_ge(row_bc_loaded, 16 * (3 * layer + 3))
                for t in range(HALVES):
                    dve.wait_ge(bank_free[t], jobs[t].at())

                stored = Count()

                def gate(i, convert=True, first=False):
                    for t in range(HALVES):
                        cols = bass.ds(i * CW, CW)
                        job_done(t)
                        if last_layer and not first:
                            dve.wait_ge(out_stored[t], stored.at(16))
                        dve.tensor_tensor(row[:, t, :], ps[:, G[t], :], gbc[:, cols], ALU.add).then_inc(bank_free[t], 1)
                        todo = (5 if t == 0 else 3) if convert else 0
                        sigs.add()
                        dve.wait_ge(sig_done, sigs.at())
                        proj = m[:, 0, cols] if t == 0 else proj1[:, cols]
                        link(dve.tensor_tensor(row[:, t, :], row[:, t, :], proj, ALU.mult))
                        dve.tensor_tensor(row[:, t, :], row[:, t, :], h[:, t, cols], ALU.add).then_inc(row_done, 1)
                        rows_out.add()
                        for _ in range(todo):
                            lo()
                        if not last_layer:
                            sq.add()
                            dve.wait_ge(split_hi_done, split_n.add())
                            b = T[(split_n.base - 1) % 2]
                            tok = slice(t * P, (t + 1) * P)
                            for k in range(4):
                                kt = bass.ds(i * 4 + k, 1)
                                last = dve.scalar_tensor_tensor(
                                    xl[:, kt, tok], ps[:, b, k * P:(k + 1) * P].unsqueeze(1),
                                    gt[:, bass.ds(i * 4 + (16 + k), 1)], xh[:, kt, tok].bitcast(F32),
                                    ALU.mult, ALU.subtract)
                            last.then_inc(split_lo_done, 1)
                    if last_layer and not first:
                        stored.add(16)

                if not last_layer:
                    with repeat(dve, 4, {**lo_steps(), sq: 2, split_n: 2, rows_out: 2, steps: 2, sigs: 2}) as i:
                        gate(i)
                    for t in range(HALVES):
                        variance(N_PRE1, t, 4, D)
                        inverse_root(N_PRE1, t)
                else:
                    gate(0, first=True)
                    with repeat(dve, 2, {**lo_steps(), rows_out: 2, steps: 2, sigs: 2, stored: 16}) as i:
                        gate(i + 1)
                    gate(3, convert=False)

            block_rest(0)

            with repeat(dve, 8, {**lo_steps(), rows_out: 2, steps: 6}):
                for t in range(HALVES):
                    skip_job(t)
                    dve.wait_ge(bank_free[t], jobs[t].at())
                    rope(t, 0, 4, 64, cos128, sin128)
                    for _ in range(5 if t == 0 else 3):
                        lo()
            with repeat(dve, 3, lo_steps()):
                for t in range(HALVES):
                    skip_job(t)
                    for _ in range(5 if t == 0 else 3):
                        lo()
            skip_job(0)
            skip_job(1)
            heads = [(MOBA_D ** -0.5, mask_causal, None, hd) for hd in range(MOBA_H)]
            for pairs, step in ODD_START:
                for _ in range(pairs):
                    lo()
                attention(SWA_H + MLA_H, heads, range(step, step + 1))
            attention(SWA_H + MLA_H, heads, range(len(ODD_START), len(heads) + 4))
            for _ in range(8 - sum(pairs for pairs, _ in ODD_START)):
                lo()
            block_rest(1)
            assert conv.base == PAIRS


_OUT = (1, SEQ, D)


def _pairs(w):
    k, n = w.shape
    return w.reshape(k // 256, 2, P, n // CW, CW).transpose(3, 0, 2, 1, 4).reshape(-1, P, 2 * CW)


def _padded(w):
    full = np.zeros((w.shape[0], CW), w.dtype)
    full[:, :w.shape[1]] = w
    return _pairs(full)


def _mlp_pairs(up, down):
    parts = []
    for g in range(GROUPS):
        parts += [_pairs(up[:, g * D:(g + 1) * D]), _pairs(down[g * D:(g + 1) * D, :])]
    return parts


def _stream(w_in, q_up, kv_up, even_out, qkv, odd_out, mlp_up, mlp_down, ple_proj, ple_gate):
    o_kr = 2 * RANK
    o_qs = o_kr + ROPE
    o_ks = o_qs + SWA_H * SWA_D
    o_vs = o_ks + SWA_KV * SWA_D
    parts = [_pairs(w_in[:, 0:2 * RANK]), _pairs(w_in[:, o_qs:o_ks]),
             _padded(np.concatenate([w_in[:, o_ks:o_vs], w_in[:, o_kr:o_qs], w_in[:, o_vs:]], axis=1))]
    q = q_up.reshape(RANK, MLA_H, NOPE + ROPE)
    for c in range(MLA_H // 2):
        a, b = 2 * c, 2 * c + 1
        parts.append(_padded(np.concatenate([q[:, a, :NOPE], q[:, b, :NOPE], q[:, a, NOPE:], q[:, b, NOPE:]], axis=1)))
    kv = kv_up.reshape(RANK, MLA_H, 2, 128)
    for c in range(MLA_H // 2):
        a, b = 2 * c, 2 * c + 1
        parts.append(_pairs(np.concatenate([kv[:, a, 0], kv[:, b, 0], kv[:, a, 1], kv[:, b, 1]], axis=1)))
    parts.append(_pairs(np.concatenate([even_out[MLA_H * 128:], even_out[:MLA_H * 128]])))
    parts += _mlp_pairs(mlp_up[0], mlp_down[0]) + [_pairs(ple_proj[0]), _pairs(ple_gate[0])]
    parts += [_pairs(qkv), _pairs(odd_out)]
    parts += _mlp_pairs(mlp_up[1], mlp_down[1]) + [_pairs(ple_proj[1]), _pairs(ple_gate[1])]
    return np.concatenate(parts)


def _by_k(v):
    return v.reshape(-1, P).T


def kernel(x, p, positions, even_pre_g, even_w_in, mla_q_norm_g, mla_w_q_up, mla_kv_norm_g, mla_w_kv_up,
           swa_sinks, even_w_out, even_post_g, odd_pre_g, moba_w_qkv, odd_w_out, odd_post_g, mlp_pre_g,
           mlp_w_up, mlp_w_down, mlp_post_g, ple_w_gate, ple_b_gate, ple_w_proj):
    import concourse.bacc as bacc
    from concourse.bass_utils import run_bass_kernel_spmd

    a = lambda v: np.asarray(v)
    x2 = a(x)[0]
    half = np.arange(64, dtype=np.float64)
    arrays = {
        "x": x2,
        "x_t": x2.T.reshape(KT, P, SEQ).transpose(1, 0, 2),
        "p_t": a(p)[:, 0].transpose(0, 2, 1).reshape(2, 2, P, SEQ).transpose(0, 2, 1, 3),
        "pos": a(positions)[0].reshape(HALVES, P).T,
        "gains_t": np.concatenate([_by_k(a(g)) for g in (even_pre_g[0], odd_pre_g[0], mlp_pre_g[0], mlp_pre_g[1],
                                                         mla_q_norm_g[0], mla_kv_norm_g[0])], axis=1),
        "rows": np.stack([a(g) for g in (even_post_g[0], mlp_post_g[0], ple_b_gate[0],
                                         odd_post_g[0], mlp_post_g[1], ple_b_gate[1])]),
        "sinks": a(swa_sinks)[0],
        "freqs": np.concatenate([THETA ** (-half * (2.0 / MOBA_D)), THETA ** (-half[:32] * (2.0 / ROPE))])
                   .astype(np.float32),
        "w_stream": _stream(a(even_w_in)[0], a(mla_w_q_up)[0], a(mla_w_kv_up)[0], a(even_w_out)[0],
                            a(moba_w_qkv)[0], a(odd_w_out)[0], a(mlp_w_up), a(mlp_w_down),
                            a(ple_w_proj), a(ple_w_gate)),
    }
    arrays = {f"in_{n}": np.ascontiguousarray(v) for n, v in arrays.items()}
    nc = bacc.Bacc("TRN2", target_bir_lowering=False, num_devices=1)
    args = [nc.dram_tensor(n, v.shape, mybir.dt.from_np(v.dtype), kind="ExternalInput").ap()
            for n, v in arrays.items()]
    out = nc.dram_tensor("out", (SEQ, D), F32, kind="ExternalOutput").ap()
    build(nc, *args, out)
    r = run_bass_kernel_spmd(nc, [arrays], core_ids=[0])
    return r.results[0]["out"].reshape(_OUT)
```
